# Optimizing a Trainium2 kernel written in Bass

```python
import math
import jax, jax.numpy as jnp
from jax import lax
import numpy as np

D_MODEL = 1024
BATCH = 1
SEQ = 512
DEPTH = 2

GRID_W = 64
CTX_LEN = 256
EPS = 1e-6
N_MOD = 6

FNET_GROUPS = 4
FNET_GROUP_DIM = 128
FNET_WIDTH = FNET_GROUPS * FNET_GROUP_DIM

SSD_HEADS = 16
SSD_HEAD_DIM = 64
SSD_INNER = SSD_HEADS * SSD_HEAD_DIM
SSD_GROUPS = 4
SSD_STATE = 128
SSD_CONV = 5
SSD_CHUNK = 128
SSD_CONV_DIM = SSD_INNER + 2 * SSD_GROUPS * SSD_STATE
EVEN_IN = FNET_WIDTH + SSD_INNER + SSD_CONV_DIM + 2 * SSD_HEADS
EVEN_OUT = FNET_WIDTH + SSD_INNER

MLA_HEADS = 16
MLA_NOPE = 64
MLA_ROPE = 32
MLA_QK = MLA_NOPE + MLA_ROPE
MLA_V = 64
MLA_Q_LORA = 384
MLA_KV_LORA = 256
ODD_IN = MLA_Q_LORA + MLA_KV_LORA + MLA_ROPE
ROPE_THETA = 10000.0
Q_BLOCK = 128

PEER_HEADS = 8
PEER_KEYS = 128
PEER_EXPERTS = PEER_KEYS * PEER_KEYS
PEER_QDIM = 256
PEER_TOPK = 16
PEER_TOKEN_BLOCK = 128

kernel_name = "hybrid_fnet_ssd_mla_peer_dit_block"

def rms_norm(x, g):
    xf = x.astype(jnp.float32)
    y = xf * lax.rsqrt(jnp.mean(xf * xf, axis=-1, keepdims=True) + EPS)
    return (y * g.astype(jnp.float32)).astype(x.dtype)

def ada_params(cond, w_ada, b_ada):
    mod = jax.nn.silu(cond) @ w_ada + b_ada
    return jnp.split(mod[..., None, :], N_MOD, axis=-1)

def modulate(x, g, shift, scale):
    return rms_norm(x, g) * (1 + scale) + shift

def fourier_mix(f):
    b, l, _ = f.shape
    fg = f.astype(jnp.float32).reshape(b, l, FNET_GROUPS, FNET_GROUP_DIM)
    out = jnp.fft.fft2(fg, axes=(1, 3), norm="ortho").real
    return out.reshape(b, l, FNET_WIDTH).astype(f.dtype)

def centred_dwconv(u, w, bias):
    pad = SSD_CONV // 2
    y = lax.conv_general_dilated(
        u, w[:, None, :].astype(u.dtype), window_strides=(1,), padding=[(pad, pad)],
        dimension_numbers=("NWC", "WIO", "NWC"), feature_group_count=u.shape[-1])
    return y + bias

def ssd_chunked(x, dt, a, bm, cm, h0):
    b, l, h, p = x.shape
    g, n = bm.shape[2], bm.shape[3]
    r = h // g
    nc, cl = l // SSD_CHUNK, SSD_CHUNK
    xd = (x.astype(jnp.float32) * dt[..., None]).reshape(b, nc, cl, g, r, p)
    a_cs = jnp.cumsum((dt * a).reshape(b, nc, cl, g, r), axis=2)
    bc = bm.astype(jnp.float32).reshape(b, nc, cl, g, n)
    cc = cm.astype(jnp.float32).reshape(b, nc, cl, g, n)
    tri = (jnp.arange(cl)[:, None] >= jnp.arange(cl)[None, :])[None, None, :, :, None, None]
    seg = a_cs[:, :, :, None] - a_cs[:, :, None, :]
    decay = jnp.exp(jnp.where(tri, seg, -jnp.inf))
    cb = jnp.einsum("bclgn,bcsgn->bclsg", cc, bc)
    y_diag = jnp.einsum("bclsgr,bcsgrp->bclgrp", cb[..., None] * decay, xd)
    to_end = jnp.exp(a_cs[:, :, -1:] - a_cs)
    states = jnp.einsum("bclgn,bclgr,bclgrp->bcgrpn", bc, to_end, xd)
    chunk_decay = jnp.exp(a_cs[:, :, -1])

    def step(hs, inp):
        s, d = inp
        return hs * d[..., None, None] + s, hs

    h_fin, h_prev = lax.scan(step, h0, (jnp.moveaxis(states, 1, 0), jnp.moveaxis(chunk_decay, 1, 0)))
    h_prev = jnp.moveaxis(h_prev, 0, 1)
    y_off = jnp.einsum("bclgn,bcgrpn,bclgr->bclgrp", cc, h_prev, jnp.exp(a_cs))
    return (y_diag + y_off).reshape(b, l, h, p), h_fin

def split_xbc(u):
    b, l, _ = u.shape
    gn = SSD_GROUPS * SSD_STATE
    xs = u[..., :SSD_INNER].reshape(b, l, SSD_HEADS, SSD_HEAD_DIM)
    bm = u[..., SSD_INNER:SSD_INNER + gn].reshape(b, l, SSD_GROUPS, SSD_STATE)
    cm = u[..., SSD_INNER + gn:].reshape(b, l, SSD_GROUPS, SSD_STATE)
    return xs, bm, cm

def ssd_bidir(u_ctx, u_lat, dt_ctx, dt_lat, p):
    a = -jnp.exp(p["a_log"].astype(jnp.float32))
    dt_bias = p["dt_bias"].astype(jnp.float32)
    d_skip = p["d_skip"].astype(jnp.float32)
    xc, bc, cc = split_xbc(u_ctx)
    xl, bl, cl = split_xbc(u_lat)
    b = u_lat.shape[0]
    y_ctx, y_lat = 0.0, 0.0
    for d in range(2):
        flip = (lambda t: jnp.flip(t, axis=1)) if d == 1 else (lambda t: t)
        dtc = jax.nn.softplus(dt_ctx[:, :, d].astype(jnp.float32) + dt_bias[d])
        dtl = jax.nn.softplus(dt_lat[:, :, d].astype(jnp.float32) + dt_bias[d])
        h0 = jnp.zeros((b, SSD_GROUPS, SSD_HEADS // SSD_GROUPS, SSD_HEAD_DIM, SSD_STATE), jnp.float32)
        yc, hc = ssd_chunked(flip(xc), flip(dtc), a[d], flip(bc), flip(cc), h0)
        yl, _ = ssd_chunked(flip(xl), flip(dtl), a[d], flip(bl), flip(cl), hc)
        y_ctx = y_ctx + flip(yc) + d_skip[d][:, None] * xc.astype(jnp.float32)
        y_lat = y_lat + flip(yl) + d_skip[d][:, None] * xl.astype(jnp.float32)
    return y_ctx, y_lat

def even_mixer(h_lat, h_ctx, p, need_ctx):
    def parts(h):
        pr = h @ p["w_in"]
        o1 = FNET_WIDTH
        o2 = o1 + SSD_INNER
        o3 = o2 + SSD_CONV_DIM
        dt = pr[..., o3:].reshape(pr.shape[0], pr.shape[1], 2, SSD_HEADS)
        u = jax.nn.silu(centred_dwconv(pr[..., o2:o3], p["conv_w"], p["conv_b"]))
        return pr[..., :o1], pr[..., o1:o2], u, dt

    f_l, z_l, u_l, dt_l = parts(h_lat)
    f_c, z_c, u_c, dt_c = parts(h_ctx)
    y_c, y_l = ssd_bidir(u_c, u_l, dt_c, dt_l, p)

    def ssd_out(y, z):
        b, l = z.shape[:2]
        gated = y.reshape(b, l, SSD_INNER) * jax.nn.silu(z.astype(jnp.float32))
        gs = SSD_INNER // SSD_GROUPS
        normed = rms_norm(gated.reshape(b, l, SSD_GROUPS, gs), p["ssd_norm"].reshape(SSD_GROUPS, gs))
        return normed.reshape(b, l, SSD_INNER).astype(z.dtype)

    def merge(f, y, z):
        return jnp.concatenate([fourier_mix(f), ssd_out(y, z)], axis=-1) @ p["w_out"]

    out_lat = merge(f_l, y_l, z_l)
    out_ctx = merge(f_c, y_c, z_c) if need_ctx else None
    return out_lat, out_ctx

def axial_rope(n_rows):
    rows = jnp.repeat(jnp.arange(n_rows), GRID_W)
    cols = jnp.tile(jnp.arange(GRID_W), n_rows)
    per_axis = MLA_ROPE // 2
    inv = ROPE_THETA ** (-jnp.arange(0, per_axis, 2, dtype=jnp.float32) / per_axis)
    ang = jnp.concatenate([rows[:, None] * inv, cols[:, None] * inv], axis=-1)
    return jnp.cos(ang), jnp.sin(ang)

def apply_rope(t, cos, sin):
    nope, rp = t[..., :MLA_NOPE], t[..., MLA_NOPE:]
    half = MLA_ROPE // 2
    x1, x2 = rp[..., :half], rp[..., half:]
    c, s = cos[:, None, :], sin[:, None, :]
    rot = jnp.concatenate([x1 * c - x2 * s, x1 * s + x2 * c], axis=-1)
    return jnp.concatenate([nope, rot.astype(t.dtype)], axis=-1)

def mla_q(dq, p, rope):
    b, l, _ = dq.shape
    q = (rms_norm(dq, p["q_a_norm"]) @ p["w_uq"]).reshape(b, l, MLA_HEADS, MLA_QK)
    q = rms_norm(q, p["q_norm"])
    return q if rope is None else apply_rope(q, *rope)

def mla_kv(dkv, p, rope):
    b, l, _ = dkv.shape
    kv = (rms_norm(dkv[..., :MLA_KV_LORA], p["kv_a_norm"]) @ p["w_ukv"]).reshape(b, l, MLA_HEADS, MLA_NOPE + MLA_V)
    k_pe = jnp.broadcast_to(dkv[..., None, MLA_KV_LORA:], (b, l, MLA_HEADS, MLA_ROPE))
    k = rms_norm(jnp.concatenate([kv[..., :MLA_NOPE], k_pe], axis=-1), p["k_norm"])
    if rope is not None:
        k = apply_rope(k, *rope)
    return k, kv[..., MLA_NOPE:]

def softmax_attend(q, k, v):
    s = jnp.einsum("bqhd,bkhd->bhqk", q, k).astype(jnp.float32) * (MLA_QK ** -0.5)
    pr = jax.nn.softmax(s, axis=-1).astype(v.dtype)
    return jnp.einsum("bhqk,bkhd->bqhd", pr, v)

def odd_mixer(h_lat, h_ctx, p, rope, need_ctx):
    d_l = h_lat @ p["w_dqkv"]
    q_l = mla_q(d_l[..., :MLA_Q_LORA], p, rope)
    k_l, v_l = mla_kv(d_l[..., MLA_Q_LORA:], p, rope)
    if need_ctx:
        d_c = h_ctx @ p["w_dqkv"]
        q_c = mla_q(d_c[..., :MLA_Q_LORA], p, None)
        k_c, v_c = mla_kv(d_c[..., MLA_Q_LORA:], p, None)
    else:
        k_c, v_c = mla_kv(h_ctx @ p["w_dqkv"][:, MLA_Q_LORA:], p, None)
    k_all = jnp.concatenate([k_c, k_l], axis=1)
    v_all = jnp.concatenate([v_c, v_l], axis=1)
    b, l = q_l.shape[:2]
    nb = l // Q_BLOCK
    qb = jnp.moveaxis(q_l.reshape(b, nb, Q_BLOCK, MLA_HEADS, MLA_QK), 1, 0)
    o = lax.map(lambda qi: softmax_attend(qi, k_all, v_all), qb)
    out_lat = jnp.moveaxis(o, 0, 1).reshape(b, l, MLA_HEADS * MLA_V) @ p["w_o"]
    out_ctx = None
    if need_ctx:
        o_c = softmax_attend(q_c, k_c, v_c)
        out_ctx = o_c.reshape(b, -1, MLA_HEADS * MLA_V) @ p["w_o"]
    return out_lat, out_ctx

def peer(h, p):
    t, dm = h.shape
    blocks = h.reshape(t // PEER_TOKEN_BLOCK, PEER_TOKEN_BLOCK, dm)

    def one(hb):
        q = (hb @ p["peer_wq"]).reshape(PEER_TOKEN_BLOCK, PEER_HEADS, 2, PEER_QDIM // 2)
        s = jnp.einsum("thsd,hskd->thsk", q, p["peer_keys"]).astype(jnp.float32)
        s_top, i_top = lax.top_k(s, PEER_TOPK)
        cand = (s_top[:, :, 0, :, None] + s_top[:, :, 1, None, :]).reshape(
            PEER_TOKEN_BLOCK, PEER_HEADS, PEER_TOPK * PEER_TOPK)
        g_score, c_idx = lax.top_k(cand, PEER_TOPK)
        e1 = jnp.take_along_axis(i_top[:, :, 0], c_idx // PEER_TOPK, axis=-1)
        e2 = jnp.take_along_axis(i_top[:, :, 1], c_idx % PEER_TOPK, axis=-1)
        experts = e1 * PEER_KEYS + e2
        gates = jax.nn.softmax(g_score, axis=-1)
        u = jnp.take(p["peer_u"], experts, axis=0)
        act = jax.nn.gelu(jnp.einsum("thkd,td->thk", u, hb).astype(jnp.float32), approximate=False) * gates
        v = jnp.take(p["peer_v"], experts, axis=0)
        return jnp.einsum("thk,thkd->td", act.astype(v.dtype), v)

    return lax.map(one, blocks).reshape(t, dm)

def setup_inputs(seed: int = 0) -> dict:
    key = jax.random.key(seed)
    ks = iter(jax.random.split(key, 64))

    def nrm(shape, scale):
        return jax.random.normal(next(ks), shape, jnp.float32) * scale

    def gain(n):
        return 1.0 + nrm((n,), 0.02)

    inp = {}
    inp["x"] = nrm((BATCH, SEQ, D_MODEL), 1.0)
    inp["c"] = nrm((BATCH, D_MODEL), 1.0)
    inp["ctx"] = nrm((BATCH, CTX_LEN, D_MODEL), 1.0)
    inp["c_ctx"] = nrm((D_MODEL,), 1.0)
    for i in range(DEPTH):
        pre = "l%d_" % i
        inp[pre + "w_ada"] = nrm((D_MODEL, N_MOD * D_MODEL), 0.5 * D_MODEL ** -0.5)
        inp[pre + "b_ada"] = nrm((N_MOD * D_MODEL,), 0.02)
        inp[pre + "norm1"] = gain(D_MODEL)
        if i % 2 == 0:
            inp[pre + "w_in"] = nrm((D_MODEL, EVEN_IN), D_MODEL ** -0.5)
            inp[pre + "conv_w"] = nrm((SSD_CONV, SSD_CONV_DIM), SSD_CONV ** -0.5)
            inp[pre + "conv_b"] = nrm((SSD_CONV_DIM,), 0.02)
            dt0 = jnp.exp(jax.random.uniform(next(ks), (2, SSD_HEADS)) * (math.log(0.1) - math.log(0.001))
                          + math.log(0.001))
            inp[pre + "dt_bias"] = dt0 + jnp.log(-jnp.expm1(-dt0))
            inp[pre + "a_log"] = jnp.log(jax.random.uniform(next(ks), (2, SSD_HEADS), minval=1.0, maxval=16.0))
            inp[pre + "d_skip"] = 1.0 + nrm((2, SSD_HEADS), 0.1)
            inp[pre + "ssd_norm"] = gain(SSD_INNER)
            inp[pre + "w_out"] = nrm((EVEN_OUT, D_MODEL), EVEN_OUT ** -0.5)
        else:
            inp[pre + "w_dqkv"] = nrm((D_MODEL, ODD_IN), D_MODEL ** -0.5)
            inp[pre + "q_a_norm"] = gain(MLA_Q_LORA)
            inp[pre + "kv_a_norm"] = gain(MLA_KV_LORA)
            inp[pre + "w_uq"] = nrm((MLA_Q_LORA, MLA_HEADS * MLA_QK), MLA_Q_LORA ** -0.5)
            inp[pre + "w_ukv"] = nrm((MLA_KV_LORA, MLA_HEADS * (MLA_NOPE + MLA_V)), MLA_KV_LORA ** -0.5)
            inp[pre + "q_norm"] = gain(MLA_QK)
            inp[pre + "k_norm"] = gain(MLA_QK)
            inp[pre + "w_o"] = nrm((MLA_HEADS * MLA_V, D_MODEL), (MLA_HEADS * MLA_V) ** -0.5)
        inp[pre + "norm2"] = gain(D_MODEL)
        inp[pre + "peer_wq"] = nrm((D_MODEL, PEER_HEADS * PEER_QDIM), D_MODEL ** -0.5)
        inp[pre + "peer_keys"] = nrm((PEER_HEADS, 2, PEER_KEYS, PEER_QDIM // 2), (PEER_QDIM // 2) ** -0.5)
        inp[pre + "peer_u"] = nrm((PEER_EXPERTS, D_MODEL), D_MODEL ** -0.5)
        inp[pre + "peer_v"] = nrm((PEER_EXPERTS, D_MODEL), 1.0)
    return inp

def reference(x, c, ctx, c_ctx,
              l0_w_ada, l0_b_ada, l0_norm1, l0_w_in, l0_conv_w, l0_conv_b, l0_dt_bias, l0_a_log,
              l0_d_skip, l0_ssd_norm, l0_w_out, l0_norm2, l0_peer_wq, l0_peer_keys, l0_peer_u, l0_peer_v,
              l1_w_ada, l1_b_ada, l1_norm1, l1_w_dqkv, l1_q_a_norm, l1_kv_a_norm, l1_w_uq, l1_w_ukv,
              l1_q_norm, l1_k_norm, l1_w_o, l1_norm2, l1_peer_wq, l1_peer_keys, l1_peer_u, l1_peer_v):
    layers = (
        dict(w_ada=l0_w_ada, b_ada=l0_b_ada, norm1=l0_norm1, w_in=l0_w_in, conv_w=l0_conv_w, conv_b=l0_conv_b,
             dt_bias=l0_dt_bias, a_log=l0_a_log, d_skip=l0_d_skip, ssd_norm=l0_ssd_norm, w_out=l0_w_out,
             norm2=l0_norm2, peer_wq=l0_peer_wq, peer_keys=l0_peer_keys, peer_u=l0_peer_u, peer_v=l0_peer_v),
        dict(w_ada=l1_w_ada, b_ada=l1_b_ada, norm1=l1_norm1, w_dqkv=l1_w_dqkv, q_a_norm=l1_q_a_norm,
             kv_a_norm=l1_kv_a_norm, w_uq=l1_w_uq, w_ukv=l1_w_ukv, q_norm=l1_q_norm, k_norm=l1_k_norm,
             w_o=l1_w_o, norm2=l1_norm2, peer_wq=l1_peer_wq, peer_keys=l1_peer_keys, peer_u=l1_peer_u,
             peer_v=l1_peer_v),
    )
    b, l, dm = x.shape
    n_rows = l // GRID_W
    rope = axial_rope(n_rows)
    x_lat, x_ctx = x, ctx
    for i in range(DEPTH):
        p = layers[i]
        need_ctx = i < DEPTH - 1
        sh1, sc1, g1, sh2, sc2, g2 = ada_params(c, p["w_ada"], p["b_ada"])
        csh1, csc1, cg1, csh2, csc2, cg2 = ada_params(c_ctx, p["w_ada"], p["b_ada"])
        h_lat = modulate(x_lat, p["norm1"], sh1, sc1)
        h_ctx = modulate(x_ctx, p["norm1"], csh1, csc1)
        if i % 2 == 0:
            y_lat, y_ctx = even_mixer(h_lat, h_ctx, p, need_ctx)
        else:
            y_lat, y_ctx = odd_mixer(h_lat, h_ctx, p, rope, need_ctx)
        x_lat = x_lat + g1 * y_lat
        h2_lat = modulate(x_lat, p["norm2"], sh2, sc2)
        if need_ctx:
            x_ctx = x_ctx + cg1 * y_ctx
            h2_ctx = modulate(x_ctx, p["norm2"], csh2, csc2)
            tokens = jnp.concatenate([h2_lat.reshape(-1, dm), h2_ctx.reshape(-1, dm)], axis=0)
            ff = peer(tokens, p)
            x_lat = x_lat + g2 * ff[: b * l].reshape(b, l, dm)
            x_ctx = x_ctx + cg2 * ff[b * l:].reshape(b, -1, dm)
        else:
            x_lat = x_lat + g2 * peer(h2_lat.reshape(-1, dm), p).reshape(b, l, dm)
    return x_lat


_drawn_inputs = setup_inputs


def setup_inputs(seed=0):
    import zlib

    import numpy as np

    out = dict(_drawn_inputs(seed))
    spreads = {}
    factors = {'l1_norm1': 8.0,
     'l1_q_a_norm': 8.0,
     'l1_kv_a_norm': 7.863,
     'l1_q_norm': 8.0,
     'l1_k_norm': 8.0,
     'l1_norm2': 6.288}
    for name, (base, spread) in spreads.items():
        noise = np.random.default_rng([zlib.crc32(name.encode()), seed]).standard_normal(out[name].shape)
        drawn = base * np.exp(spread * noise) if base else spread * noise
        out[name] = __import__('jax').numpy.asarray(drawn.astype(out[name].dtype))
    for name, factor in factors.items():
        out[name] = (out[name] * factor).astype(out[name].dtype)
    return out
```

```python
from contextlib import ExitStack

import concourse.bass as bass
from concourse import mybir

F32 = mybir.dt.float32
U32 = mybir.dt.uint32
ALU = mybir.AluOpType
ACT = mybir.ActivationFunctionType
AX_X = mybir.AxisListType.X

P = 128
D = 1024
KD = D // P
LAT, CTX = 512, 256
TL, TC = LAT // P, CTX // P
TT = TL + TC
TOK = LAT + CTX
EPS = 1e-6

GROUPS, GDIM = 4, 128
FW = GROUPS * GDIM
HEADS, HD = 16, 64
INNER = HEADS * HD
SG, SN = 4, 128
HG = HEADS // SG
GW = HG * HD
TAPS = 5
CONV = INNER + 2 * SG * SN
EVEN_IN = FW + INNER + CONV + 2 * HEADS
EVEN_OUT = FW + INNER

MH, NOPE, ROPE, MV = 16, 64, 32, 64
QK = NOPE + ROPE
QL, KVL = 384, 256
ODD_IN = QL + KVL + ROPE

PH, PK, PQ, TOPK = 8, 128, 256, 16
EXPERTS = PK * PK
LOWEST = -3.0e38

C_ID, C_TRI, C_NEG, C_ONE, C_DFT, C_IOTA = 0, 128, 384, 640, 768, 1024
C_WORDS = 1040
S_COND = 1040
S_MOD = 1056
S_NORM = S_MOD + 128
S_BASE = S_NORM + 32
XO = 2048
RO = XO + TT * D
SLOT = 4096
HO = RO + 3 * SLOT
L0 = HO + KD * TOK
MISC = L0 + 24576
WORDS = 53208



def up(sig, n=1):
    sig["total"] += n
    return n


def at(sig, n):
    return sig["base"] + n


def signal(core, name):
    if name not in core["signals"]:
        core["signals"][name] = {"sem": core["ctx"].enter_context(core["nc"].semaphore(name)),
                                 "base": 0, "total": 0}
    return core["signals"][name]


def close(core):
    for name in core["signals"]:
        core["signals"][name]["base"] = core["signals"][name]["total"]


def view(core, start, *shape):
    n = 1
    for s in shape:
        n *= s
    v = core["sb"][:, start:start + n]
    if len(shape) == 2:
        v = v.rearrange("p (a b) -> p a b", b=shape[1])
    if len(shape) == 3:
        v = v.rearrange("p (a b c) -> p a b c", b=shape[1], c=shape[2])
    return v


def pair(core, b):
    return core["ps"][:, b:b + 2, :].rearrange("p a b -> p (a b)")


def ident(core):
    return view(core, C_ID, P)


def ring_plan(core, chunks, slots=3):
    plan = []
    uses = [0] * slots
    for c in range(chunks):
        s = c % slots
        uses[s] += 1
        plan.append((s, core["ring"][s], at(core["ring"][s], 16 * uses[s])))
    return plan


def bcast(ap, n):
    return ap.unsqueeze(2).to_broadcast([ap.shape[0], ap.shape[1], n])


def load_constants(core, d):
    nc = core["nc"]
    loaded = signal(core, "constants_loaded")
    silu_done = signal(core, "cond_silu_done")
    cond = view(core, S_COND, KD, 2)
    with nc.Block() as block:
        @block.sync
        def _(sp):
            sp.dma_start(view(core, 0, C_WORDS), d["const"]).then_inc(loaded["sem"], up(loaded, 16))
            sp.dma_start(view(core, S_COND, KD * 2), d["cond"]).then_inc(loaded["sem"], up(loaded, 16))
            sp.dma_start(view(core, S_NORM, 4 * KD), d["norms"]).then_inc(loaded["sem"], up(loaded, 16))
            sp.dma_start(view(core, XO, TL, D),
                         d["x"].rearrange("(t p) n -> p t n", p=P)).then_inc(loaded["sem"], up(loaded, 16))
            sp.dma_start(view(core, XO + TL * D, TC, D),
                         d["ctx"].rearrange("(t p) n -> p t n", p=P)).then_inc(loaded["sem"], up(loaded, 16))
            sp.wait_ge(loaded["sem"], at(loaded, 80))

        @block.scalar
        def _(act):
            act.wait_ge(loaded["sem"], at(loaded, 80))
            act.activation(cond, cond, ACT.Silu).then_inc(silu_done["sem"], up(silu_done))
    close(core)


def ada_stage(core, d, layer):
    nc = core["nc"]
    N = 6 * D // 512
    plan = ring_plan(core, N)
    cond = view(core, S_COND, KD, 2)
    bias = view(core, L0, 6 * D)[0:2]
    row = view(core, HO, 6 * D)[0:2]
    cols = view(core, S_MOD + layer * 64, 4, KD * 2)
    norms = view(core, S_NORM + layer * 2 * KD, 2, KD)
    b_in = signal(core, "ada_bias_loaded")
    mm = signal(core, "ada_product_done")
    add = signal(core, "ada_bias_added")
    tr = signal(core, "ada_columns_turned")
    own = signal(core, "ada_columns_step")
    st = signal(core, "gates_stored")
    w = d[f"l{layer}_w_ada"].rearrange("(k p) n -> p k n", p=P)
    with nc.Block() as block:
        @block.sync
        def _(sp):
            sp.dma_start(bias, d[f"l{layer}_b_ada"].to_broadcast([2, 6 * D])).then_inc(b_in["sem"], up(b_in, 16))
            for c, (s, sig, _v) in enumerate(plan):
                if c >= 3:
                    sp.wait_ge(mm["sem"], at(mm, c - 2))
                sp.dma_start(view(core, RO + s * SLOT, KD, 512),
                             w[:, :, c * 512:(c + 1) * 512]).then_inc(sig["sem"], up(sig, 16))
            sp.wait_ge(add["sem"], at(add, N))
            for kind, start in ((0, 2 * D), (1, 5 * D)):
                sp.dma_start(d["gates"][layer, kind], row[:, start:start + D]).then_inc(st["sem"], up(st, 16))
            sp.wait_ge(st["sem"], at(st, 32))

        @block.tensor
        def _(pe):
            for c, (s, sig, v) in enumerate(plan):
                pe.wait_ge(sig["sem"], v)
                if c >= 4:
                    pe.wait_ge(add["sem"], at(add, c - 3))
                wt = view(core, RO + s * SLOT, KD, 512)
                for k in range(KD):
                    i = pe.matmul(core["ps"][0:2, c % 4, :], cond[:, k, :], wt[:, k, :],
                                  start=(k == 0), stop=(k == KD - 1))
                i.then_inc(mm["sem"], up(mm))
            pe.wait_ge(add["sem"], at(add, N))
            for j, part in enumerate((1, 0, 4, 3)):
                for k in range(KD):
                    i = pe.transpose(core["ps"][:, 4, (j * KD + k) * 2:(j * KD + k) * 2 + 2],
                                     row[:, part * D + k * P:part * D + (k + 1) * P],
                                     ident(core)[0:2, 0:2])
            i.then_inc(tr["sem"], up(tr))

        @block.vector
        def _(dve):
            dve.wait_ge(b_in["sem"], at(b_in, 16))
            for c in range(N):
                dve.wait_ge(mm["sem"], at(mm, c + 1))
                dve.tensor_tensor(row[:, c * 512:(c + 1) * 512], core["ps"][0:2, c % 4, :],
                                  bias[:, c * 512:(c + 1) * 512], ALU.add).then_inc(add["sem"], up(add))
            dve.wait_ge(tr["sem"], at(tr, 1))
            dve.tensor_copy(cols.rearrange("p a b -> p (a b)"),
                            core["ps"][:, 4, 0:8 * KD]).then_inc(own["sem"], up(own))
            dve.wait_ge(own["sem"], own["total"])
            for n in range(2):
                c2 = cols[:, 2 * n, :].rearrange("p (k c) -> p k c", c=2)
                dve.scalar_tensor_tensor(out=c2, in0=c2, scalar=1.0, in1=bcast(norms[:, n, :], 2),
                                         op0=ALU.add, op1=ALU.mult).then_inc(own["sem"], up(own))
    close(core)


def norm_stage(core, layer, which, tiles, h2=None):
    nc = core["nc"]
    x = view(core, XO, TT, D)
    ht = view(core, HO, KD, TOK)
    squares = view(core, RO, D)
    xn = view(core, RO + D, 2, D)
    ss = view(core, MISC, TT)
    rstd = view(core, MISC + 8, TT)
    scale = view(core, S_MOD + layer * 64 + which * 32, KD, 2)
    shift = view(core, S_MOD + layer * 64 + which * 32 + 16, KD, 2)
    sq = signal(core, "norm_squares_summed")
    root = signal(core, "norm_root_done")
    own = signal(core, "norm_rows_ready")
    tr = signal(core, "norm_rows_turned")
    cola = signal(core, "norm_low_columns_out")
    colv = signal(core, "norm_high_columns_out")
    back = signal(core, "norm_columns_turned_back")
    out = signal(core, "norm_h2_out")
    st = signal(core, "norm_h2_stored")
    with nc.Block() as block:
        @block.sync
        def _(sp):
            if h2 is None:
                return
            for t in range(tiles):
                sp.wait_ge(out["sem"], at(out, t + 1))
                sp.dma_start(core["h2_rows"][t], h2[:, t, :]).then_inc(st["sem"], up(st, 16))
            sp.wait_ge(st["sem"], st["total"])

        @block.scalar
        def _(act):
            for t in range(tiles):
                if t:
                    act.wait_ge(sq["sem"], sq["total"])
                act.activation(squares, x[:, t, :], ACT.Square,
                               accum_out=ss[:, t:t + 1]).then_inc(sq["sem"], up(sq))
            act.wait_ge(own["sem"], at(own, 1))
            act.activation(rstd[:, 0:tiles], ss[:, 0:tiles], ACT.Sqrt).then_inc(root["sem"], up(root))
            for t in range(tiles):
                c = 0 if t < TL else 1
                act.wait_ge(tr["sem"], at(tr, t + 1))
                for k in range(KD // 2):
                    i = act.activation(ht[:, k, t * P:(t + 1) * P],
                                       pair(core, 2 * (t % 2))[:, k * P:(k + 1) * P], ACT.Identity,
                                       bias=shift[:, k, c:c + 1], scale=scale[:, k, c:c + 1])
                i.then_inc(cola["sem"], up(cola))

        @block.vector
        def _(dve):
            dve.wait_ge(sq["sem"], at(sq, tiles))
            dve.tensor_scalar(ss[:, 0:tiles], ss[:, 0:tiles], 1.0 / D, EPS, ALU.mult,
                              ALU.add).then_inc(own["sem"], up(own))
            dve.wait_ge(root["sem"], at(root, 1))
            dve.reciprocal(rstd[:, 0:tiles], rstd[:, 0:tiles]).then_inc(own["sem"], up(own))
            dve.wait_ge(own["sem"], own["total"])
            for t in range(tiles + 2):
                if t < tiles:
                    if t >= 2:
                        dve.wait_ge(tr["sem"], at(tr, t - 1))
                    dve.tensor_scalar(xn[:, t % 2, :], x[:, t, :], rstd[:, t:t + 1], None,
                                      ALU.mult).then_inc(own["sem"], up(own))
                if 1 <= t <= tiles:
                    u = t - 1
                    c = 0 if u < TL else 1
                    dve.wait_ge(tr["sem"], at(tr, u + 1))
                    for k in range(KD // 2, KD):
                        i = dve.tensor_scalar(ht[:, k, u * P:(u + 1) * P],
                                              pair(core, 2 * (u % 2))[:, k * P:(k + 1) * P],
                                              scale[:, k, c:c + 1], shift[:, k, c:c + 1],
                                              ALU.mult, ALU.add)
                    i.then_inc(colv["sem"], up(colv))
                if t >= 2 and h2 is not None:
                    u = t - 2
                    dve.wait_ge(back["sem"], at(back, u + 1))
                    dve.tensor_copy(h2[:, u, :], pair(core, 4 + 2 * (u % 2))).then_inc(out["sem"], up(out))

        @block.tensor
        def _(pe):
            for t in range(tiles + 1):
                if t < tiles:
                    pe.wait_ge(own["sem"], at(own, t + 3))
                    if t >= 2:
                        pe.wait_ge(cola["sem"], at(cola, t - 1))
                        pe.wait_ge(colv["sem"], at(colv, t - 1))
                    for k in range(KD):
                        i = pe.transpose(pair(core, 2 * (t % 2))[:, k * P:(k + 1) * P],
                                         xn[:, t % 2, k * P:(k + 1) * P], ident(core))
                    i.then_inc(tr["sem"], up(tr))
                if t >= 1 and h2 is not None:
                    u = t - 1
                    pe.wait_ge(cola["sem"], at(cola, u + 1))
                    pe.wait_ge(colv["sem"], at(colv, u + 1))
                    if u >= 2:
                        pe.wait_ge(out["sem"], at(out, u - 1))
                    for k in range(KD):
                        i = pe.transpose(pair(core, 4 + 2 * (u % 2))[:, k * P:(k + 1) * P],
                                         ht[:, k, u * P:(u + 1) * P], ident(core))
                    i.then_inc(back["sem"], up(back))
    close(core)


FT_O = L0
ZS_O = FT_O + GROUPS * TOK
BC_O = ZS_O + TT * INNER
XS_O = BC_O + 2 * SG * TOK
BR_O = XS_O + TT * INNER
SEG = 2 + LAT + 2 + 2 + CTX + 2
CO = LAT + 4
S_CW = S_BASE
S_DTR = S_BASE + 96


def project_stage(core, d):
    nc = core["nc"]
    ht = view(core, HO, KD, TOK)
    ft = view(core, FT_O, GROUPS, TOK)
    zs = view(core, ZS_O, TT, INNER)
    bct = view(core, BC_O, 2 * SG, TOK)
    xs = view(core, XS_O, TT, INNER)
    br = view(core, BR_O, TT, SG * SN)
    cw = view(core, S_CW, 16, TAPS)
    cb = view(core, S_CW + 80, 16)
    dtr = view(core, S_DTR, TT, 2 * HEADS)
    pad = [view(core, RO + 2 * SLOT, SEG), view(core, RO + 2 * SLOT + SEG, SEG)]
    acc = [view(core, RO + 2 * SLOT + 2 * SEG, SEG), view(core, RO + 2 * SLOT + 3 * SEG, SEG)]
    sil = [view(core, MISC, TOK), view(core, MISC + TOK, TOK)]
    w = d["l0_w_in"].rearrange("(k p) n -> p k n", p=P)
    UT = (FW + CONV) // P
    starts = [0] + [FW + INNER + 512 * c for c in range(4)] + [FW, FW + 512, EVEN_IN - 2 * HEADS]
    widths = [512] * 7 + [2 * HEADS]
    plan = ring_plan(core, 8, 2)
    taps_in = signal(core, "conv_taps_loaded")
    zero = signal(core, "conv_pads_zeroed")
    mm = signal(core, "project_product_done")
    ev = signal(core, "project_banks_read")
    cv = signal(core, "conv_step")
    si = signal(core, "conv_silu_done")
    tr = signal(core, "conv_columns_turned")
    rw = signal(core, "conv_rows_out")
    NF, NU = GROUPS, UT
    NR = 12

    with nc.Block() as block:
        @block.sync
        def _(sp):
            sp.dma_start(view(core, S_CW, 96), d["conv"]).then_inc(taps_in["sem"], up(taps_in, 16))
            for c, (s, sig, _v) in enumerate(plan):
                if c >= 2:
                    q = c - 2
                    n = 4 * (q + 1) if q < 5 else NU + 6 * (q - 4)
                    sp.wait_ge(mm["sem"], at(mm, n))
                sp.dma_start(view(core, RO + s * SLOT, KD, 512)[:, :, 0:widths[c]],
                             w[:, :, starts[c]:starts[c] + widths[c]]).then_inc(sig["sem"], up(sig, 16))

        @block.gpsimd
        def _(pool):
            for b in range(2):
                pool.memset(pad[b], 0.0).then_inc(zero["sem"], up(zero))

        @block.tensor
        def _(pe):
            def turn(u):
                v = u - NF
                pe.wait_ge(si["sem"], at(si, v + 1))
                if v >= 2:
                    pe.wait_ge(rw["sem"], at(rw, v - 1))
                for t in range(TT):
                    i = pe.transpose(pair(core, 4 + 2 * (v % 2))[:, t * P:(t + 1) * P],
                                     sil[v % 2][:, t * P:(t + 1) * P] if v < 8 else
                                     bct[:, v - 8, t * P:(t + 1) * P], ident(core))
                i.then_inc(tr["sem"], up(tr))

            for u in range(NU):
                s, sig, v = plan[u // 4]
                if u % 4 == 0:
                    pe.wait_ge(sig["sem"], v)
                if u >= 2:
                    pe.wait_ge(ev["sem"], at(ev, u - 1))
                wt = view(core, RO + s * SLOT, KD, 512)
                o = pair(core, 2 * (u % 2))
                for a, b in ((0, LAT), (LAT, TOK)):
                    for k in range(KD):
                        i = pe.matmul(o[:, a:b], wt[:, k, (u % 4) * P:(u % 4 + 1) * P], ht[:, k, a:b],
                                      start=(k == 0), stop=(k == KD - 1))
                i.then_inc(mm["sem"], up(mm))
                if NF <= u - 2 < NF + NR:
                    turn(u - 2)
            n = 0
            for c in range(5, 8):
                s, sig, v = plan[c]
                pe.wait_ge(sig["sem"], v)
                wt = view(core, RO + s * SLOT, KD, 512)
                for t in range(TT):
                    pe.wait_ge(ev["sem"], at(ev, NU + n - 3 if n >= 4 else NU))
                    for k in range(KD):
                        i = pe.matmul(core["ps"][:, n % 4, 0:widths[c]], ht[:, k, t * P:(t + 1) * P],
                                      wt[:, k, 0:widths[c]], start=(k == 0), stop=(k == KD - 1))
                    i.then_inc(mm["sem"], up(mm))
                    n += 1

        @block.scalar
        def _(act):
            def silu(u):
                v = u - NF
                act.wait_ge(cv["sem"], at(cv, TAPS * (v + 1)))
                if v < 8:
                    if v >= 2:
                        act.wait_ge(tr["sem"], at(tr, v - 1))
                    o = sil[v % 2]
                else:
                    o = bct[:, v - 8, :]
                act.activation(o[:, 0:LAT], acc[v % 2][:, 0:LAT], ACT.Silu)
                act.activation(o[:, LAT:TOK], acc[v % 2][:, CO:CO + CTX],
                               ACT.Silu).then_inc(si["sem"], up(si))

            act.wait_ge(zero["sem"], at(zero, 2))
            for u in range(NU):
                act.wait_ge(mm["sem"], at(mm, u + 1))
                o = pair(core, 2 * (u % 2))
                if u < NF:
                    act.activation(ft[:, u, :], o[:, 0:TOK], ACT.Copy).then_inc(ev["sem"], up(ev))
                    continue
                v = u - NF
                if v >= 2:
                    act.wait_ge(cv["sem"], at(cv, TAPS * (v - 1)))
                act.activation(pad[v % 2][:, 2:2 + LAT], o[:, 0:LAT], ACT.Copy)
                act.activation(pad[v % 2][:, CO + 2:CO + 2 + CTX], o[:, LAT:TOK],
                               ACT.Copy).then_inc(ev["sem"], up(ev))
                if v >= 1:
                    silu(u - 1)
            silu(NU - 1)
            for n in range(3 * TT):
                act.wait_ge(mm["sem"], at(mm, NU + n + 1))
                t = n % TT
                if n < 2 * TT:
                    c = n // TT
                    act.activation(zs[:, t, c * 512:(c + 1) * 512], core["ps"][:, n % 4, :],
                                   ACT.Silu).then_inc(ev["sem"], up(ev))
                else:
                    act.activation(dtr[:, t, :], core["ps"][:, n % 4, 0:2 * HEADS],
                                   ACT.Copy).then_inc(ev["sem"], up(ev))

        @block.vector
        def _(dve):
            W = SEG - 4
            def rows(v):
                dve.wait_ge(tr["sem"], at(tr, v + 1))
                o = (xs[:, :, v * P:(v + 1) * P] if v < 8 else br[:, :, (v - 8) * P:(v - 7) * P])
                dve.tensor_copy(o, pair(core, 4 + 2 * (v % 2))[:, 0:TOK].rearrange(
                    "p (t n) -> p t n", n=P)).then_inc(rw["sem"], up(rw))

            dve.wait_ge(taps_in["sem"], at(taps_in, 16))
            for v in range(NU - NF):
                dve.wait_ge(ev["sem"], at(ev, NF + v + 1))
                if v >= 2:
                    dve.wait_ge(si["sem"], at(si, v - 1))
                a = acc[v % 2]
                dve.tensor_scalar(a[:, 0:W], pad[v % 2][:, 0:W], cw[:, v, 0:1], cb[:, v:v + 1],
                                  ALU.mult, ALU.add).then_inc(cv["sem"], up(cv))
                for j in range(1, TAPS):
                    dve.wait_ge(cv["sem"], cv["total"])
                    dve.scalar_tensor_tensor(out=a[:, 0:W], in0=pad[v % 2][:, j:j + W],
                                             scalar=cw[:, v, j:j + 1], in1=a[:, 0:W],
                                             op0=ALU.mult, op1=ALU.add).then_inc(cv["sem"], up(cv))
                if 2 <= v < NR + 2:
                    rows(v - 2)
    close(core)


def fourier_stage(core, d):
    nc = core["nc"]
    ft = view(core, FT_O, GROUPS, TOK)
    uv = view(core, RO, TT, GROUPS * 2 * GDIM)[:, :, :]
    cl = view(core, RO + 6144, TL, 2 * LAT)
    cc = view(core, RO + 6144 + TL * 2 * LAT, TC, 2 * CTX)
    dft = view(core, C_DFT, 2 * GDIM)
    tab = signal(core, "dft_tables_loaded")
    mm = signal(core, "dft_channels_done")
    ev = signal(core, "dft_channels_out")
    pm = signal(core, "dft_positions_done")
    po = signal(core, "dft_positions_out")
    N = TT * 2
    with nc.Block() as block:
        @block.sync
        def _(sp):
            sp.dma_start(cl, d["dft_lat"].rearrange("(t p) n -> p t n", p=P)).then_inc(tab["sem"], up(tab, 16))
            sp.dma_start(cc, d["dft_ctx"].rearrange("(t p) n -> p t n", p=P)).then_inc(tab["sem"], up(tab, 16))

        @block.tensor
        def _(pe):
            for n in range(N):
                if n >= 4:
                    pe.wait_ge(ev["sem"], at(ev, n - 3))
                t = n // 2
                for j in range(2):
                    i = pe.matmul(core["ps"][:, n % 4, j * 256:(j + 1) * 256],
                                  ft[:, 2 * (n % 2) + j, t * P:(t + 1) * P], dft, start=True, stop=True)
                i.then_inc(mm["sem"], up(mm))
            pe.wait_ge(tab["sem"], at(tab, 32))
            pe.wait_ge(ev["sem"], at(ev, N))
            for n in range(2 * GROUPS):
                g = n // 2
                tiles, first, tb, L = ((TL, 0, cl, LAT), (TC, TL, cc, CTX))[n % 2]
                if n >= 4:
                    pe.wait_ge(po["sem"], at(po, n - 3))
                for t in range(tiles):
                    for part in range(2):
                        i = pe.matmul(core["ps"][:, 4 + n % 4, 0:L],
                                      uv[:, first + t, g * 256 + part * P:g * 256 + (part + 1) * P],
                                      tb[:, t, part * L:(part + 1) * L],
                                      start=(t == 0 and part == 0), stop=(t == tiles - 1 and part == 1))
                i.then_inc(pm["sem"], up(pm))

        @block.vector
        def _(dve):
            for n in range(N):
                dve.wait_ge(mm["sem"], at(mm, n + 1))
                dve.tensor_copy(uv[:, n // 2, (n % 2) * 512:(n % 2 + 1) * 512],
                                core["ps"][:, n % 4, :]).then_inc(ev["sem"], up(ev))
            for n in range(2 * GROUPS):
                dve.wait_ge(pm["sem"], at(pm, n + 1))
                a, L = ((0, LAT), (LAT, CTX))[n % 2]
                dve.tensor_copy(ft[:, n // 2, a:a + L], core["ps"][:, 4 + n % 4, 0:L]).then_inc(po["sem"], up(po))
    close(core)


def ssd_stage(core, d):
    nc = core["nc"]
    y = view(core, HO, TT, INNER)
    bct = view(core, BC_O, 2 * SG, TOK)
    xs = view(core, XS_O, TT, INNER)
    br = view(core, BR_O, TT, SG * SN)
    dtr = view(core, S_DTR, TT, 2 * HEADS)
    E = view(core, RO, 2, 512)
    M = view(core, RO + 1024, 2, 512)
    XD = view(core, RO + 2048, 2, GW)
    XE = view(core, RO + 2560, 2, GW)
    TMP = view(core, RO + 3072, GW)
    HS = view(core, RO + 3328, 2, INNER)
    rows = view(core, RO + 5376, 5, 32)
    W = TT * 2 * HEADS
    DT, DTA, ACS, EAC, NAC, TOE, CD, T0, T1 = (view(core, RO + 5536 + i * W, TT, 2 * HEADS) for i in range(9))
    flat = lambda v: v.rearrange("p a b -> p (a b)")
    tri = view(core, C_TRI, 2, P)
    neg = view(core, C_NEG, 2, P)
    ones = view(core, C_ONE, P)
    ld = signal(core, "ssd_rows_loaded")
    ex = signal(core, "ssd_prepare_act")
    pr = signal(core, "ssd_prepare_dve")
    sm = signal(core, "ssd_sums_done")
    fr = signal(core, "ssd_scores_done")
    eo = signal(core, "ssd_decay_ready")
    mo = signal(core, "ssd_masked_ready")
    xo = signal(core, "ssd_inputs_ready")
    bk = signal(core, "ssd_products_done")
    ac = signal(core, "ssd_added")
    order = [[4, 5, 0, 1, 2, 3], [5, 4, 3, 2, 1, 0]]
    steps = [(r, t, g) for r in range(2) for t in order[r] for g in range(SG)]
    NS = len(steps)
    with nc.Block() as block:
        @block.sync
        def _(sp):
            sp.dma_start(flat(rows[:, 0:3, :]), d["ssd_rows"].to_broadcast([P, 96])).then_inc(ld["sem"], up(ld, 16))

        @block.scalar
        def _(act):
            act.wait_ge(ld["sem"], at(ld, 16))
            act.activation(rows[:, 3, :], rows[:, 1, :], ACT.Exp).then_inc(ex["sem"], up(ex))
            act.wait_ge(pr["sem"], at(pr, 2))
            act.activation(flat(T1), flat(T1), ACT.Exp).then_inc(ex["sem"], up(ex))
            act.wait_ge(ex["sem"], ex["total"])
            act.activation(flat(T1), flat(T1), ACT.Ln, bias=1.0).then_inc(ex["sem"], up(ex))
            act.wait_ge(pr["sem"], at(pr, 8))
            act.activation(flat(EAC), flat(ACS), ACT.Exp).then_inc(ex["sem"], up(ex))
            act.activation(flat(TOE), flat(TOE), ACT.Exp).then_inc(ex["sem"], up(ex))
            act.activation(flat(CD), flat(CD), ACT.Exp).then_inc(ex["sem"], up(ex))
            for n, (r, t, g) in enumerate(steps):
                act.wait_ge(fr["sem"], at(fr, n + 1))
                if n >= 2:
                    act.wait_ge(mo["sem"], at(mo, n - 1))
                for h in range(HG):
                    c = r * HEADS + g * HG + h
                    i = act.activation(E[:, n % 2, h * P:(h + 1) * P], core["ps"][:, n % 2, h * P:(h + 1) * P],
                                       ACT.Exp, bias=NAC[:, t, c:c + 1])
                i.then_inc(eo["sem"], up(eo))

        @block.vector
        def _(dve):
            dve.wait_ge(ld["sem"], at(ld, 16))
            dve.tensor_tensor(T0, dtr, rows[:, 0:1, :].to_broadcast([P, TT, 32]),
                              ALU.add).then_inc(pr["sem"], up(pr))
            dve.wait_ge(pr["sem"], pr["total"])
            dve.scalar_tensor_tensor(out=flat(T1), in0=flat(T0), scalar=-1.0, in1=flat(T0),
                                     op0=ALU.mult, op1=ALU.min).then_inc(pr["sem"], up(pr))
            dve.wait_ge(ex["sem"], at(ex, 3))
            dve.scalar_tensor_tensor(out=flat(DT), in0=flat(T0), scalar=0.0, in1=flat(T1),
                                     op0=ALU.max, op1=ALU.add).then_inc(pr["sem"], up(pr))
            dve.wait_ge(pr["sem"], pr["total"])
            dve.scalar_tensor_tensor(out=DTA, in0=DT, scalar=-1.0,
                                     in1=rows[:, 3:4, :].to_broadcast([P, TT, 32]),
                                     op0=ALU.mult, op1=ALU.mult).then_inc(pr["sem"], up(pr))
            dve.wait_ge(sm["sem"], at(sm, 1))
            for r in range(2):
                i = dve.tensor_copy(ACS[:, :, r * HEADS:(r + 1) * HEADS],
                                    core["ps"][:, r, 0:W].rearrange("p (a b) -> p a b", b=32)
                                    [:, :, r * HEADS:(r + 1) * HEADS])
            i.then_inc(pr["sem"], up(pr))
            dve.tensor_copy(flat(CD), core["ps"][:, 2, 0:W]).then_inc(pr["sem"], up(pr))
            dve.wait_ge(pr["sem"], pr["total"])
            dve.tensor_tensor(flat(TOE), flat(CD), flat(ACS), ALU.subtract).then_inc(pr["sem"], up(pr))
            dve.tensor_scalar(flat(NAC), flat(ACS), -1.0, None, ALU.mult).then_inc(pr["sem"], up(pr))
            dve.tensor_tensor(rows[:, 4, 0:16], rows[:, 2, 0:16], rows[:, 2, 16:32],
                              ALU.add).then_inc(pr["sem"], up(pr))
            dve.memset(flat(HS), 0.0).then_inc(pr["sem"], up(pr))
            dve.wait_ge(pr["sem"], pr["total"])
            for t in range(TT):
                dve.tensor_tensor(y[:, t, :].rearrange("p (h c) -> p h c", c=HD),
                                  xs[:, t, :].rearrange("p (h c) -> p h c", c=HD),
                                  bcast(rows[:, 4, 0:16], HD), ALU.mult).then_inc(pr["sem"], up(pr))
            dve.wait_ge(ex["sem"], at(ex, 6))

            def mask(n):
                dve.wait_ge(eo["sem"], at(eo, n + 1))
                dve.wait_ge(fr["sem"], at(fr, n + 1))
                if n >= 2:
                    dve.wait_ge(bk["sem"], at(bk, n - 1))
                sc = core["ps"][:, 2 + n % 2, 0:P].unsqueeze(1).to_broadcast([P, HG, P])
                dve.tensor_tensor(M[:, n % 2, :].rearrange("p (h l) -> p h l", l=P),
                                  E[:, n % 2, :].rearrange("p (h l) -> p h l", l=P), sc,
                                  ALU.mult).then_inc(mo["sem"], up(mo))

            def add(n):
                r, t, g = steps[n]
                c = r * HEADS + g * HG
                yg = y[:, t, g * GW:(g + 1) * GW]
                hs = HS[:, r, g * GW:(g + 1) * GW]
                per = lambda v: v.rearrange("p (h c) -> p h c", c=HD)
                dve.wait_ge(bk["sem"], at(bk, n + 1))
                if n:
                    dve.wait_ge(ac["sem"], ac["total"])
                dve.tensor_tensor(per(TMP), per(core["ps"][:, 4 + n % 2, GW:2 * GW]),
                                  bcast(EAC[:, t, c:c + HG], HD), ALU.mult).then_inc(ac["sem"], up(ac))
                dve.tensor_tensor(yg, yg, core["ps"][:, 4 + n % 2, 0:GW], ALU.add).then_inc(ac["sem"], up(ac))
                dve.tensor_tensor(per(hs), per(hs), bcast(CD[:, t, c:c + HG], HD),
                                  ALU.mult).then_inc(ac["sem"], up(ac))
                dve.wait_ge(ac["sem"], ac["total"])
                dve.tensor_tensor(yg, yg, TMP, ALU.add).then_inc(ac["sem"], up(ac))
                dve.tensor_tensor(hs, hs, core["ps"][:, 6 + n % 2, 0:GW], ALU.add).then_inc(ac["sem"], up(ac))

            dve.wait_ge(pr["sem"], pr["total"])
            mask(0)
            for n in range(NS):
                if n + 1 < NS:
                    mask(n + 1)
                add(n)

        @block.gpsimd
        def _(pool):
            pool.wait_ge(pr["sem"], at(pr, 3))
            pool.wait_ge(ex["sem"], at(ex, 6))
            for n, (r, t, g) in enumerate(steps):
                c = r * HEADS + g * HG
                per = lambda v: v.rearrange("p (h c) -> p h c", c=HD)
                if n >= 2:
                    pool.wait_ge(bk["sem"], at(bk, n - 1))
                pool.tensor_tensor(per(XD[:, n % 2, :]), per(xs[:, t, g * GW:(g + 1) * GW]),
                                   bcast(DT[:, t, c:c + HG], HD), ALU.mult).then_inc(xo["sem"], up(xo))
                pool.wait_ge(xo["sem"], xo["total"])
                pool.tensor_tensor(per(XE[:, n % 2, :]), per(XD[:, n % 2, :]),
                                   bcast(TOE[:, t, c:c + HG], HD), ALU.mult).then_inc(xo["sem"], up(xo))

        @block.tensor
        def _(pe):
            pe.wait_ge(pr["sem"], at(pr, 4))
            for b, m in enumerate((tri[:, 0, :], tri[:, 1, :], ones)):
                i = pe.matmul(core["ps"][:, b, 0:W], m, flat(DTA), start=True, stop=True)
            i.then_inc(sm["sem"], up(sm))
            pe.wait_ge(pr["sem"], at(pr, 6))

            def front(n):
                r, t, g = steps[n]
                if n >= 2:
                    pe.wait_ge(eo["sem"], at(eo, n - 1))
                    pe.wait_ge(mo["sem"], at(mo, n - 1))
                pe.matmul(core["ps"][:, 2 + n % 2, 0:P], bct[:, g, t * P:(t + 1) * P],
                          bct[:, SG + g, t * P:(t + 1) * P], start=True, stop=True)
                for h in range(HG):
                    c = r * HEADS + g * HG + h
                    o = core["ps"][:, n % 2, h * P:(h + 1) * P]
                    pe.matmul(o, DTA[:, t, c:c + 1].to_broadcast([P, P]), tri[:, r, :],
                              start=True, stop=False)
                    i = pe.matmul(o, ident(core), neg[:, r, :], start=False, stop=True)
                i.then_inc(fr["sem"], up(fr))

            front(0)
            for n, (r, t, g) in enumerate(steps):
                if n + 1 < NS:
                    front(n + 1)
                pe.wait_ge(mo["sem"], at(mo, n + 1))
                pe.wait_ge(xo["sem"], at(xo, 2 * n + 2))
                if n >= 4:
                    pe.wait_ge(ac["sem"], at(ac, 5 * (n - 3)))
                else:
                    pe.wait_ge(pr["sem"], at(pr, 10))
                    if n >= 2:
                        pe.wait_ge(ac["sem"], at(ac, 5 * (n - 1)))
                if n >= 4:
                    pe.wait_ge(ac["sem"], at(ac, 5 * (n - 1)))
                for h in range(HG):
                    pe.matmul(core["ps"][:, 4 + n % 2, h * HD:(h + 1) * HD], M[:, n % 2, h * P:(h + 1) * P],
                              XD[:, n % 2, h * HD:(h + 1) * HD], start=True, stop=True)
                pe.matmul(core["ps"][:, 4 + n % 2, GW:2 * GW], bct[:, SG + g, t * P:(t + 1) * P],
                          HS[:, r, g * GW:(g + 1) * GW], start=True, stop=True)
                pe.matmul(core["ps"][:, 6 + n % 2, 0:GW], br[:, t, g * SN:(g + 1) * SN], XE[:, n % 2, :],
                          start=True, stop=True).then_inc(bk["sem"], up(bk))
    close(core)


def gate_stage(core, d):
    nc = core["nc"]
    y = view(core, HO, TT, INNER)
    zs = view(core, ZS_O, TT, INNER)
    ms = view(core, BC_O, KD, TOK)
    sq = view(core, RO, INNER)
    ss = view(core, S_BASE, TT * SG)
    rstd = view(core, S_BASE + 32, TT * SG)
    gain = view(core, S_BASE + 64, KD)
    ld = signal(core, "ssd_gain_loaded")
    gt = signal(core, "gate_rows_step")
    qs = signal(core, "gate_squares_summed")
    tr = signal(core, "gate_rows_turned")
    ca = signal(core, "gate_low_columns_out")
    cv = signal(core, "gate_high_columns_out")
    with nc.Block() as block:
        @block.sync
        def _(sp):
            sp.dma_start(gain, d["ssd_norm"]).then_inc(ld["sem"], up(ld, 16))

        @block.vector
        def _(dve):
            for t in range(TT):
                dve.tensor_tensor(y[:, t, :], y[:, t, :], zs[:, t, :], ALU.mult).then_inc(gt["sem"], up(gt))
            dve.wait_ge(qs["sem"], at(qs, TT))
            dve.tensor_scalar(ss, ss, 1.0 / GW, EPS, ALU.mult, ALU.add).then_inc(gt["sem"], up(gt))
            dve.wait_ge(qs["sem"], at(qs, TT + 1))
            dve.reciprocal(rstd, rstd).then_inc(gt["sem"], up(gt))
            dve.wait_ge(gt["sem"], gt["total"])
            dve.wait_ge(ld["sem"], at(ld, 16))
            for t in range(TT + 1):
                if t < TT:
                    yt = y[:, t, :].rearrange("p (g c) -> p g c", c=GW)
                    dve.tensor_tensor(yt, yt, bcast(rstd[:, t * SG:(t + 1) * SG], GW),
                                      ALU.mult).then_inc(gt["sem"], up(gt))
                if t >= 1:
                    u = t - 1
                    dve.wait_ge(tr["sem"], at(tr, u + 1))
                    for k in range(KD // 2, KD):
                        i = dve.tensor_scalar(ms[:, k, u * P:(u + 1) * P],
                                              pair(core, 2 * (u % 2))[:, k * P:(k + 1) * P],
                                              gain[:, k:k + 1], None, ALU.mult)
                    i.then_inc(cv["sem"], up(cv))

        @block.scalar
        def _(act):
            for t in range(TT):
                act.wait_ge(gt["sem"], at(gt, t + 1))
                if t:
                    act.wait_ge(qs["sem"], qs["total"])
                for g in range(SG):
                    i = act.activation(sq[:, g * GW:(g + 1) * GW], y[:, t, g * GW:(g + 1) * GW], ACT.Square,
                                       accum_out=ss[:, t * SG + g:t * SG + g + 1])
                i.then_inc(qs["sem"], up(qs))
            act.wait_ge(gt["sem"], at(gt, TT + 1))
            act.activation(rstd, ss, ACT.Sqrt).then_inc(qs["sem"], up(qs))
            act.wait_ge(ld["sem"], at(ld, 16))
            for t in range(TT):
                act.wait_ge(tr["sem"], at(tr, t + 1))
                for k in range(KD // 2):
                    i = act.activation(ms[:, k, t * P:(t + 1) * P],
                                       pair(core, 2 * (t % 2))[:, k * P:(k + 1) * P], ACT.Copy,
                                       scale=gain[:, k:k + 1])
                i.then_inc(ca["sem"], up(ca))

        @block.tensor
        def _(pe):
            for t in range(TT):
                pe.wait_ge(gt["sem"], at(gt, TT + 3 + t))
                if t >= 2:
                    pe.wait_ge(ca["sem"], at(ca, t - 1))
                    pe.wait_ge(cv["sem"], at(cv, t - 1))
                for k in range(KD):
                    i = pe.transpose(pair(core, 2 * (t % 2))[:, k * P:(k + 1) * P],
                                     y[:, t, k * P:(k + 1) * P], ident(core))
                i.then_inc(tr["sem"], up(tr))
    close(core)


def out_stage(core, weights, lhs, wcols, gates, layer, tiles):
    nc = core["nc"]
    K = weights.shape[0] // P
    x = view(core, XO, TT, D)
    w = weights.rearrange("(k p) n -> p k n", p=P)
    gr = view(core, gates, 2, D)
    prod = view(core, MISC, 2, 512)
    ld = [signal(core, f"out_weights{c}_loaded") for c in range(2)]
    gl = signal(core, "out_gates_loaded")
    mm = signal(core, "out_product_done")
    gd = signal(core, "out_gated")
    ad = signal(core, "out_added")
    with nc.Block() as block:
        @block.sync
        def _(sp):
            for c in range(2):
                sp.dma_start(wcols(c), w[:, :, c * 512:(c + 1) * 512]).then_inc(ld[c]["sem"], up(ld[c], 16))
            for n in range(2):
                sp.dma_start(gr[:, n, :], core["gates"][layer, 0, n:n + 1, :].to_broadcast([P, D])
                             ).then_inc(gl["sem"], up(gl, 16))

        @block.tensor
        def _(pe):
            n = 0
            for c in range(2):
                pe.wait_ge(ld[c]["sem"], at(ld[c], 16))
                for t in range(tiles):
                    if n >= 4:
                        pe.wait_ge(gd["sem"], at(gd, n - 3))
                    for k in range(K):
                        i = pe.matmul(core["ps"][:, n % 4, :], lhs(k, t), wcols(c)[:, k, :],
                                      start=(k == 0), stop=(k == K - 1))
                    i.then_inc(mm["sem"], up(mm))
                    n += 1

        @block.vector
        def _(dve):
            dve.wait_ge(gl["sem"], at(gl, 32))
            n = 0
            for c in range(2):
                for t in range(tiles):
                    s = slice(c * 512, (c + 1) * 512)
                    dve.wait_ge(mm["sem"], at(mm, n + 1))
                    if n >= 2:
                        dve.wait_ge(ad["sem"], at(ad, n - 1))
                    dve.tensor_tensor(prod[:, n % 2, :], core["ps"][:, n % 4, :],
                                      gr[:, 0 if t < TL else 1, s], ALU.mult).then_inc(gd["sem"], up(gd))
                    dve.wait_ge(gd["sem"], gd["total"])
                    dve.tensor_tensor(x[:, t, s], x[:, t, s], prod[:, n % 2, :],
                                      ALU.add).then_inc(ad["sem"], up(ad))
                    n += 1
    close(core)


KT_O = HO
V_O = KT_O + MH * TOK
QT_O = V_O + TT * D
T_O = QT_O + MH * LAT
OT_O = QT_O
DN_O = HO + KD * TOK
S_KPE = S_BASE
S_AN = S_BASE + 192
S_SS = S_BASE + 200
S_RS = S_BASE + 216


def mla_down_stage(core, d):
    nc = core["nc"]
    ht = view(core, HO, KD, TOK)
    dn = view(core, DN_O, TT, ODD_IN)
    w = view(core, RO, KD, ODD_IN)
    sq = view(core, RO + KD * ODD_IN, QL)
    kpe = view(core, S_KPE, TT, ROPE)
    an = view(core, S_AN, 5)
    ss = view(core, S_SS, TT, 2)
    rs = view(core, S_RS, TT, 2)
    qat = view(core, T_O, 3, LAT)
    kvt = view(core, T_O + 3 * LAT, 2, TOK)
    ld = signal(core, "down_weights_loaded")
    mm = signal(core, "down_product_done")
    ev = signal(core, "down_rows_out")
    qs = signal(core, "down_squares_summed")
    st = signal(core, "down_rows_step")
    tr = signal(core, "down_rows_turned")
    co = signal(core, "down_columns_out")
    with nc.Block() as block:
        @block.sync
        def _(sp):
            sp.dma_start(w, d["l1_w_dqkv"].rearrange("(k p) n -> p k n", p=P)).then_inc(ld["sem"], up(ld, 16))
            sp.dma_start(an, d["a_norms"]).then_inc(ld["sem"], up(ld, 16))

        @block.tensor
        def _(pe):
            pe.wait_ge(ld["sem"], at(ld, 32))
            for t in range(TT):
                if t >= 2:
                    pe.wait_ge(ev["sem"], at(ev, t - 1))
                o = pair(core, 2 * (t % 2))
                for a, b in ((0, 512), (512, ODD_IN)):
                    for k in range(KD):
                        i = pe.matmul(o[:, a:b], ht[:, k, t * P:(t + 1) * P], w[:, k, a:b],
                                      start=(k == 0), stop=(k == KD - 1))
                i.then_inc(mm["sem"], up(mm))
            for t in range(TT):
                pe.wait_ge(st["sem"], at(st, 3 + 2 * t + 2))
                if t >= 2:
                    pe.wait_ge(co["sem"], at(co, t - 1))
                for k in range(5):
                    if k < 3 and t >= TL:
                        continue
                    i = pe.transpose(pair(core, 4 + 2 * (t % 2))[:, k * P:(k + 1) * P],
                                     dn[:, t, k * P:(k + 1) * P], ident(core))
                i.then_inc(tr["sem"], up(tr))

        @block.scalar
        def _(act):
            for t in range(TT):
                act.wait_ge(ev["sem"], at(ev, t + 1))
                for j, (a, b) in enumerate(((0, QL), (QL, QL + KVL))):
                    if t or j:
                        act.wait_ge(qs["sem"], qs["total"])
                    act.activation(sq[:, 0:b - a], dn[:, t, a:b], ACT.Square,
                                   accum_out=ss[:, t, j:j + 1]).then_inc(qs["sem"], up(qs))
            act.wait_ge(st["sem"], at(st, 2))
            act.activation(rs.rearrange("p a b -> p (a b)"), ss.rearrange("p a b -> p (a b)"),
                           ACT.Sqrt).then_inc(qs["sem"], up(qs))
            for t in range(TT):
                act.wait_ge(tr["sem"], at(tr, t + 1))
                for k in range(5):
                    if k < 3 and t >= TL:
                        continue
                    o = qat[:, k, t * P:(t + 1) * P] if k < 3 else kvt[:, k - 3, t * P:(t + 1) * P]
                    i = act.activation(o, pair(core, 4 + 2 * (t % 2))[:, k * P:(k + 1) * P], ACT.Copy,
                                       scale=an[:, k:k + 1])
                i.then_inc(co["sem"], up(co))

        @block.vector
        def _(dve):
            for t in range(TT):
                dve.wait_ge(mm["sem"], at(mm, t + 1))
                dve.tensor_copy(dn[:, t, :], pair(core, 2 * (t % 2))[:, 0:ODD_IN]).then_inc(ev["sem"], up(ev))
            dve.wait_ge(qs["sem"], at(qs, 2 * TT))
            dve.tensor_scalar(ss[:, :, 0:1], ss[:, :, 0:1], 1.0 / QL, EPS, ALU.mult,
                              ALU.add).then_inc(st["sem"], up(st))
            dve.tensor_scalar(ss[:, :, 1:2], ss[:, :, 1:2], 1.0 / KVL, EPS, ALU.mult,
                              ALU.add).then_inc(st["sem"], up(st))
            dve.wait_ge(qs["sem"], at(qs, 2 * TT + 1))
            dve.reciprocal(rs.rearrange("p a b -> p (a b)"),
                           rs.rearrange("p a b -> p (a b)")).then_inc(st["sem"], up(st))
            dve.wait_ge(st["sem"], st["total"])
            for t in range(TT):
                for j, (a, b) in enumerate(((0, QL), (QL, QL + KVL))):
                    dve.tensor_scalar(dn[:, t, a:b], dn[:, t, a:b], rs[:, t, j:j + 1], None,
                                      ALU.mult).then_inc(st["sem"], up(st))
            dve.wait_ge(ev["sem"], ev["total"])
            dve.tensor_copy(kpe, dn[:, :, QL + KVL:ODD_IN]).then_inc(st["sem"], up(st))
    close(core)


def mla_up_stage(core, d):
    nc = core["nc"]
    wq = view(core, RO, 3, MH * QK)
    wkv = view(core, RO + 3 * MH * QK, 2, MH * (NOPE + MV))
    rowb = view(core, RO + 8704, 2, MH * QK)
    kpe = view(core, S_KPE, TT, ROPE)
    qat = view(core, T_O, 3, LAT)
    kvt = view(core, T_O + 3 * LAT, 2, TOK)
    kt = view(core, KT_O, MH, TOK)
    qt = view(core, QT_O, MH, LAT)
    val = view(core, V_O, TT, D)
    sq = view(core, MISC, MH, QK)
    rot = view(core, MISC + MH * QK, MH, 16)
    ss = view(core, S_SS, MH)
    rs = view(core, S_RS, MH)
    gain = view(core, S_BASE + 240, 2, QK)
    cs = view(core, S_BASE + 240 + 2 * QK, 2, TL * 16)
    ld = signal(core, "up_weights_loaded")
    mm = signal(core, "up_product_done")
    ev = signal(core, "up_rows_out")
    st = signal(core, "up_rows_step")
    ro = signal(core, "up_root_done")
    rd = signal(core, "up_rows_ready")
    tr = signal(core, "up_rows_turned")
    co = signal(core, "up_columns_out")
    items = []
    for t in range(TT):
        items.append((0, t))
        if t < TL:
            items.append((1, t))
    per_item = []

    count = 0
    for q, t in items:
        a = count + (3 if q else 4)
        b = a + 3 + (6 if t < TL else 0)
        per_item.append((a, b))
        count = b

    with nc.Block() as block:
        @block.sync
        def _(sp):
            sp.dma_start(wkv, d["l1_w_ukv"].rearrange("(k p) n -> p k n", p=P)).then_inc(ld["sem"], up(ld, 16))
            sp.dma_start(wq, d["l1_w_uq"].rearrange("(k p) n -> p k n", p=P)).then_inc(ld["sem"], up(ld, 16))
            sp.dma_start(view(core, S_BASE + 240, 2 * QK),
                         d["qk_norms"].to_broadcast([P, 2 * QK])).then_inc(ld["sem"], up(ld, 16))
            sp.dma_start(view(core, S_BASE + 240 + 2 * QK, 2 * TL * 16), d["rope"]).then_inc(ld["sem"], up(ld, 16))

        @block.tensor
        def _(pe):
            def turn(n):
                q, t = items[n]
                pe.wait_ge(rd["sem"], at(rd, n + 1))
                if n >= 1:
                    pe.wait_ge(co["sem"], at(co, 4 * n))
                for h in range(MH):
                    i = pe.transpose(core["ps"][0:QK, 4 + h // 4, (h % 4) * P:(h % 4 + 1) * P],
                                     rowb[:, n % 2, h * QK:(h + 1) * QK], ident(core))
                    if h % 4 == 3:
                        i.then_inc(tr["sem"], up(tr))

            pe.wait_ge(ld["sem"], at(ld, 64))
            for n, (q, t) in enumerate(items):
                if n >= 1:
                    pe.wait_ge(ev["sem"], at(ev, 2 * n))
                K, a, w, C = (3, qat, wq, 3) if q else (2, kvt, wkv, 4)
                for c in range(C):
                    for k in range(K):
                        i = pe.matmul(core["ps"][:, c, :], a[:, k, t * P:(t + 1) * P],
                                      w[:, k, c * 512:(c + 1) * 512], start=(k == 0), stop=(k == K - 1))
                i.then_inc(mm["sem"], up(mm))
                if n >= 1:
                    turn(n - 1)
            turn(len(items) - 1)

        @block.scalar
        def _(act):
            def columns(n):
                q, t = items[n]
                o = qt if q else kt
                for b in range(4):
                    act.wait_ge(tr["sem"], at(tr, 4 * n + b + 1))
                    act.activation(o[0:QK, 4 * b:4 * b + 4, t * P:(t + 1) * P],
                                   core["ps"][0:QK, 4 + b, :].rearrange("p (h l) -> p h l", l=P),
                                   ACT.Copy).then_inc(co["sem"], up(co))

            for n, (q, t) in enumerate(items):
                act.wait_ge(mm["sem"], at(mm, n + 1))
                kv = core["ps"][:, 0:4, :].rearrange("p a b -> p (a b)").rearrange("p (h c) -> p h c", c=P)
                if n >= 2:
                    act.wait_ge(tr["sem"], at(tr, 4 * (n - 1)))
                row = rowb[:, n % 2, :]
                if q:
                    act.activation(row, core["ps"][:, 0:3, :].rearrange("p a b -> p (a b)"),
                                   ACT.Copy).then_inc(ev["sem"], up(ev, 2))
                else:
                    act.activation(row.rearrange("p (h c) -> p h c", c=QK)[:, :, 0:NOPE],
                                   kv[:, :, 0:NOPE], ACT.Copy).then_inc(ev["sem"], up(ev))
                    act.activation(val[:, t, :].rearrange("p (h c) -> p h c", c=MV),
                                   kv[:, :, NOPE:], ACT.Copy).then_inc(ev["sem"], up(ev))
                act.wait_ge(st["sem"], at(st, per_item[n][0]))
                act.activation(rs, ss, ACT.Sqrt).then_inc(ro["sem"], up(ro))
                if n >= 1:
                    columns(n - 1)
            columns(len(items) - 1)

        @block.vector
        def _(dve):
            dve.wait_ge(ld["sem"], at(ld, 64))
            for n, (q, t) in enumerate(items):
                row = rowb[:, n % 2, :].rearrange("p (h c) -> p h c", c=QK)
                if n >= 2:
                    dve.wait_ge(tr["sem"], at(tr, 4 * (n - 1)))
                if not q:
                    dve.tensor_copy(row[:, :, NOPE:], kpe[:, t:t + 1, :].to_broadcast([P, MH, ROPE])
                                    ).then_inc(st["sem"], up(st))
                    dve.wait_ge(st["sem"], st["total"])
                dve.wait_ge(ev["sem"], at(ev, 2 * n + 2))
                dve.tensor_tensor(sq, row, row, ALU.mult).then_inc(st["sem"], up(st))
                dve.wait_ge(st["sem"], st["total"])
                dve.tensor_reduce(ss, sq, AX_X, ALU.add).then_inc(st["sem"], up(st))
                dve.wait_ge(st["sem"], st["total"])
                dve.tensor_scalar(ss, ss, 1.0 / QK, EPS, ALU.mult, ALU.add).then_inc(st["sem"], up(st))
                dve.wait_ge(ro["sem"], at(ro, n + 1))
                dve.reciprocal(rs, rs).then_inc(st["sem"], up(st))
                dve.wait_ge(st["sem"], st["total"])
                dve.tensor_tensor(row, row, bcast(rs, QK), ALU.mult).then_inc(st["sem"], up(st))
                dve.wait_ge(st["sem"], st["total"])
                g = gain[:, 0 if q else 1:(0 if q else 1) + 1, :].to_broadcast([P, MH, QK])
                i = dve.tensor_tensor(row, row, g, ALU.mult).then_inc(st["sem"], up(st))
                if t < TL:
                    dve.wait_ge(st["sem"], st["total"])
                    x1, x2 = row[:, :, NOPE:NOPE + 16], row[:, :, NOPE + 16:]
                    c = cs[:, 0:1, t * 16:(t + 1) * 16].to_broadcast([P, MH, 16])
                    s = cs[:, 1:2, t * 16:(t + 1) * 16].to_broadcast([P, MH, 16])
                    sc = sq.rearrange("p a b -> p (a b)")
                    x1s = sc[:, 0:256].rearrange("p (h c) -> p h c", c=16)
                    x2c = sc[:, 256:512].rearrange("p (h c) -> p h c", c=16)
                    dve.tensor_tensor(rot, x2, s, ALU.mult).then_inc(st["sem"], up(st))
                    dve.tensor_tensor(x1s, x1, s, ALU.mult).then_inc(st["sem"], up(st))
                    dve.tensor_tensor(x2c, x2, c, ALU.mult).then_inc(st["sem"], up(st))
                    dve.wait_ge(st["sem"], st["total"])
                    dve.tensor_tensor(x1, x1, c, ALU.mult).then_inc(st["sem"], up(st))
                    dve.tensor_tensor(x2, x1s, x2c, ALU.add).then_inc(st["sem"], up(st))
                    dve.wait_ge(st["sem"], st["total"])
                    dve.tensor_tensor(x1, x1, rot, ALU.subtract).then_inc(st["sem"], up(st))
                assert st["total"] - st["base"] == per_item[n][1]
                dve.wait_ge(st["sem"], st["total"])
                dve.tensor_copy(rot[:, 0, 0:1], row[:, 0, 0:1]).then_inc(rd["sem"], up(rd))
    close(core)


def attention_stage(core, d):
    nc = core["nc"]
    kt = view(core, KT_O, MH, TOK)
    qt = view(core, QT_O, MH, LAT)
    val = view(core, V_O, TT, D)
    rows = view(core, RO, TL, D)
    ot = view(core, OT_O, KD, LAT)
    pr = view(core, T_O, 3, TOK)
    pt = view(core, MISC, 2, TOK)
    N = MH * TL
    top, nm, sm, rc = (view(core, S_SS + i * N, N) for i in range(4))
    sc = signal(core, "scores_ready")
    mx = signal(core, "score_peak_ready")
    ex = signal(core, "exponentials_ready")
    iv = signal(core, "softmax_sum_inverted")
    tr = signal(core, "exponentials_turned")
    pc = signal(core, "turned_exponentials_out")
    pv = signal(core, "head_output_ready")
    oo = signal(core, "head_output_out")
    tt = signal(core, "output_rows_turned")
    to = signal(core, "output_columns_out")
    scale = QK ** -0.5
    with nc.Block() as block:
        @block.tensor
        def _(pe):
            def score(n):
                h, q = divmod(n, TL)
                if n >= 2:
                    pe.wait_ge(ex["sem"], at(ex, n - 1))
                o = pair(core, 2 * (n % 2))
                for a, b in ((0, 512), (512, TOK)):
                    i = pe.matmul(o[:, a:b], qt[0:QK, h, q * P:(q + 1) * P], kt[0:QK, h, a:b],
                                  start=True, stop=True)
                i.then_inc(sc["sem"], up(sc))

            def turn(n):
                pe.wait_ge(ex["sem"], at(ex, n + 1))
                if n >= 1:
                    pe.wait_ge(pc["sem"], at(pc, n))
                for t in range(TT):
                    i = pe.transpose(pair(core, 4)[:, t * P:(t + 1) * P], pr[:, n % 3, t * P:(t + 1) * P],
                                     ident(core))
                i.then_inc(tr["sem"], up(tr))

            def weigh(n):
                h, q = divmod(n, TL)
                pe.wait_ge(pc["sem"], at(pc, n + 1))
                if n >= 2:
                    pe.wait_ge(oo["sem"], at(oo, n - 1))
                for t in range(TT):
                    i = pe.matmul(core["ps"][:, 6 + n % 2, 0:MV], pt[:, n % 2, t * P:(t + 1) * P],
                                  val[:, t, h * MV:(h + 1) * MV], start=(t == 0), stop=(t == TT - 1))
                i.then_inc(pv["sem"], up(pv))

            for n in range(N + 3):
                if n < N:
                    score(n)
                if 2 <= n < N + 2:
                    turn(n - 2)
                if n >= 3:
                    weigh(n - 3)
            pe.wait_ge(oo["sem"], at(oo, N))
            for t in range(TL):
                if t >= 2:
                    pe.wait_ge(to["sem"], at(to, t - 1))
                for k in range(KD):
                    i = pe.transpose(pair(core, 2 * (t % 2))[:, k * P:(k + 1) * P],
                                     rows[:, t, k * P:(k + 1) * P], ident(core))
                i.then_inc(tt["sem"], up(tt))

        @block.vector
        def _(dve):
            def peak(n):
                dve.wait_ge(sc["sem"], at(sc, n + 1))
                dve.tensor_reduce(top[:, n:n + 1], pair(core, 2 * (n % 2))[:, 0:TOK], AX_X,
                                  ALU.max).then_inc(mx["sem"], up(mx))
                dve.wait_ge(mx["sem"], mx["total"])
                dve.tensor_scalar(nm[:, n:n + 1], top[:, n:n + 1], -scale, None,
                                  ALU.mult).then_inc(mx["sem"], up(mx))

            def out(n):
                h, q = divmod(n, TL)
                dve.reciprocal(rc[:, n:n + 1], sm[:, n:n + 1]).then_inc(iv["sem"], up(iv))
                dve.wait_ge(iv["sem"], iv["total"])
                dve.wait_ge(pv["sem"], at(pv, n + 1))
                dve.tensor_scalar(rows[:, q, h * MV:(h + 1) * MV], core["ps"][:, 6 + n % 2, 0:MV],
                                  rc[:, n:n + 1], None, ALU.mult).then_inc(oo["sem"], up(oo))

            for n in range(N + 4):
                if n < N:
                    peak(n)
                if n >= 4:
                    dve.wait_ge(ex["sem"], at(ex, n - 3))
                    out(n - 4)

        @block.scalar
        def _(act):
            for n in range(N + 2):
                if n < N:
                    act.wait_ge(mx["sem"], at(mx, 2 * (n + 1)))
                    if n >= 3:
                        act.wait_ge(tr["sem"], at(tr, n - 2))
                    act.activation(pr[:, n % 3, :], pair(core, 2 * (n % 2))[:, 0:TOK], ACT.Exp,
                                   bias=nm[:, n:n + 1], scale=scale,
                                   accum_out=sm[:, n:n + 1]).then_inc(ex["sem"], up(ex))
                if n >= 2:
                    u = n - 2
                    act.wait_ge(tr["sem"], at(tr, u + 1))
                    if u >= 2:
                        act.wait_ge(pv["sem"], at(pv, u - 1))
                    act.activation(pt[:, u % 2, :], pair(core, 4)[:, 0:TOK],
                                   ACT.Copy).then_inc(pc["sem"], up(pc))
            for t in range(TL):
                act.wait_ge(tt["sem"], at(tt, t + 1))
                act.activation(ot[:, :, t * P:(t + 1) * P],
                               pair(core, 2 * (t % 2)).rearrange("p (k l) -> p k l", l=P),
                               ACT.Copy).then_inc(to["sem"], up(to))
    close(core)


H2_O = L0
SC_O = H2_O + TT * D
KY_O = SC_O + (TT * PH + 1) * 2 * PK
Q_O = KY_O + 2 * PH * PK
NSLOT = TOPK
ROWS = 2 * D
G2_O = RO + NSLOT * ROWS
W_O = G2_O + 2 * D
BATCH = 4


def peer_score_stage(core, d, layer, tiles):
    nc = core["nc"]
    ht = view(core, HO, KD, TOK)
    keys = view(core, KY_O, 2 * PH, PK)
    qb = view(core, Q_O, 2, TOK)
    sc = view(core, SC_O, TT * PH, 2 * PK)
    w = d[f"l{layer}_peer_wq"].rearrange("(k p) n -> p k n", p=P)
    C = PH * PQ // 512
    plan = ring_plan(core, C)
    n_tok = tiles * P
    parts = [(0, 512)] + ([(512, n_tok)] if n_tok > 512 else [])
    N = 2 * PH
    ky = signal(core, "peer_keys_loaded")
    mm = signal(core, "peer_query_done")
    qe = signal(core, "peer_query_out")
    sm = signal(core, "peer_scores_done")
    se = signal(core, "peer_scores_out")
    st = signal(core, "peer_scores_stored")
    with nc.Block() as block:
        @block.sync
        def _(sp):
            sp.dma_start(keys, d[f"keys{layer}"]).then_inc(ky["sem"], up(ky, 16))
            for c, (s, sig, _v) in enumerate(plan):
                if c >= 3:
                    sp.wait_ge(mm["sem"], at(mm, 4 * (c - 2)))
                sp.dma_start(view(core, RO + s * SLOT, KD, 512),
                             w[:, :, c * 512:(c + 1) * 512]).then_inc(sig["sem"], up(sig, 16))
            rows = core["score_rows"]
            dst = rows[0:tiles * PH].rearrange("(t h) p k -> p t h k", h=PH)
            src = sc[:, 0:tiles * PH, :].rearrange("p (t h) k -> p t h k", h=PH)
            for h in range(PH):
                sp.wait_ge(se["sem"], at(se, 2 * h + 2))
                sp.dma_start(dst[:, :, h, :], src[:, :, h, :]).then_inc(st["sem"], up(st, 16))
            sp.dma_start(rows[tiles * PH:tiles * PH + 2].rearrange("n p k -> p n k"),
                         sc[:, 0:2, :]).then_inc(st["sem"], up(st, 16))
            sp.wait_ge(st["sem"], st["total"])

        @block.tensor
        def _(pe):
            def score(n):
                pe.wait_ge(qe["sem"], at(qe, n + 1))
                if n >= 2:
                    pe.wait_ge(se["sem"], at(se, n - 1))
                for t in range(tiles):
                    i = pe.matmul(pair(core, 4 + 2 * (n % 2))[:, t * P:(t + 1) * P],
                                  qb[:, n % 2, t * P:(t + 1) * P], keys[:, n, :], start=True, stop=True)
                i.then_inc(sm["sem"], up(sm))

            pe.wait_ge(ky["sem"], at(ky, 16))
            for n in range(N):
                s, sig, v = plan[n // 4]
                if n % 4 == 0:
                    pe.wait_ge(sig["sem"], v)
                if n >= 2:
                    pe.wait_ge(qe["sem"], at(qe, n - 1))
                wt = view(core, RO + s * SLOT, KD, 512)
                for a, b in parts:
                    for k in range(KD):
                        i = pe.matmul(pair(core, 2 * (n % 2))[:, a:b], wt[:, k, (n % 4) * P:(n % 4 + 1) * P],
                                      ht[:, k, a:b], start=(k == 0), stop=(k == KD - 1))
                i.then_inc(mm["sem"], up(mm))
                if n >= 1:
                    score(n - 1)
            score(N - 1)

        @block.scalar
        def _(act):
            for n in range(N):
                act.wait_ge(mm["sem"], at(mm, n + 1))
                if n >= 2:
                    act.wait_ge(sm["sem"], at(sm, n - 1))
                act.activation(qb[:, n % 2, 0:n_tok], pair(core, 2 * (n % 2))[:, 0:n_tok],
                               ACT.Copy).then_inc(qe["sem"], up(qe))

        @block.vector
        def _(dve):
            for n in range(N):
                h, side = divmod(n, 2)
                dve.wait_ge(sm["sem"], at(sm, n + 1))
                o = sc[:, 0:tiles * PH, :].rearrange("p (t h) k -> p t h k", h=PH)
                dve.tensor_copy(o[:, :, h, side * PK:(side + 1) * PK],
                                pair(core, 4 + 2 * (n % 2))[:, 0:n_tok].rearrange("p (t k) -> p t k", k=PK)
                                ).then_inc(se["sem"], up(se))
    close(core)


def peer_gather_stage(core, d, layer, tiles):
    nc = core["nc"]
    steps = tiles * PH
    x = view(core, XO, TT * D)
    slots = view(core, RO, NSLOT, ROWS)
    g2 = view(core, G2_O, 2 * D)
    top = [W_O]

    def take(*shape):
        n = 1
        for s in shape:
            n *= s
        v = view(core, top[0], *shape)
        top[0] += n
        return v

    h = take(D)
    diag = take(BATCH * 2, P)
    gated = take(D)
    ahead = take(4, PK)
    cur2 = take(2, PK)
    best = take(2, TOPK)
    where = take(2, TOPK).bitcast(U32)
    wheref = take(2, TOPK)
    cand = take(TOPK, TOPK)
    cand2 = take(TOPK, TOPK)
    score = take(TOPK)
    pick = take(TOPK).bitcast(U32)
    halves = take(2, TOPK).bitcast(U32)
    halvesf = take(2, TOPK)
    hot = take(2 * TOPK, TOPK)
    ef = take(2 * TOPK)
    shifted = take(TOPK)
    raised = take(TOPK)
    total = take(2)
    dots = take(TOPK)
    gel = take(TOPK)
    wts = take(TOPK)
    expert = take(2, TOPK).bitcast(U32)
    gate = take(2, TOPK)
    assert top[0] <= WORDS
    iota = view(core, C_IOTA, TOPK)
    flat = lambda v: v.rearrange("p a b -> p (a b)")
    sig = lambda name: signal(core, name)
    g2l = sig("peer_gates_loaded")
    rdy = sig("peer_experts_chosen")
    cho = sig("peer_choice_step")
    ctn = sig("peer_choice_turn")
    exd = sig("peer_softmax_raised")
    hst = sig("peer_row_loaded")
    scl = [sig(f"peer_scores{n}_loaded") for n in range(2)]
    turn = sig("peer_gather_turn")
    free = sig("peer_slot_used")
    land = [sig(f"peer_slot{s}_landed") for s in range(NSLOT)]
    dot = sig("peer_dots_ready")
    gl = sig("peer_gelu_ready")
    wt = sig("peer_weights_ready")
    dg = sig("peer_diagonals_ready")
    rd = sig("peer_tile_read")
    xup = sig("peer_tile_added")
    hfree = sig("peer_row_used")
    CH = 26
    NB = TOPK // BATCH
    tbl = d[f"experts{layer}"]

    with nc.Block() as block:
        @block.sync
        def _(sp):
            for n in range(2):
                sp.dma_start(g2[:, n * D:(n + 1) * D],
                             core["gates"][layer, 1, n:n + 1, :].to_broadcast([P, D])).then_inc(g2l["sem"], up(g2l, 16))
            rows = core["score_rows"].rearrange("n p k -> p n k")
            h2 = core["h2_rows"].rearrange("t p n -> p t n")
            for n in range(2):
                sp.dma_start(flat(ahead[:, 2 * n:2 * n + 2, :]), rows[:, n, :]).then_inc(scl[n]["sem"], 16)
            with sp.Fori(0, tiles) as t:
                sp.wait_ge(hfree["sem"], t + at(hfree, 1))
                sp.dma_start(h, h2[:, bass.ds(t, 1), :].rearrange("p a n -> p (a n)")).then_inc(hst["sem"], 16)
                with sp.Fori(0, PH // 2) as hh:
                    for n in range(2):
                        i = t * PH + hh * 2 + n
                        sp.wait_ge(cho["sem"], i * CH + at(cho, CH))
                        sp.dma_start(flat(ahead[:, 2 * n:2 * n + 2, :]),
                                     rows[:, bass.ds(i + 2, 1), :].rearrange("p a k -> p (a k)")
                                     ).then_inc(scl[n]["sem"], 16)
            for n in range(2):
                sp.wait_ge(scl[n]["sem"], at(scl[n], 16 * (steps // 2 + 1)))

        @block.gpsimd
        def _(pool):
            with pool.Fori(0, steps // 2) as ii:
                for par in range(2):
                    i = ii * 2 + par
                    pool.wait_ge(rdy["sem"], i + at(rdy, 1))
                    for k in range(TOPK):
                        pool.wait_ge(free["sem"], i * TOPK + at(free, k + 1))
                        pool.sem_inc(turn["sem"], 1)
                        pool.indirect_dma_start(slots[:, k % NSLOT, :], None, tbl,
                                                bass.IndirectOffsetOnAxis(ap=expert[:, par, k:k + 1], axis=0)
                                                ).then_inc(land[k % NSLOT]["sem"], 16)

        @block.tensor
        def _(pe):
            pe.sem_inc(free["sem"], NSLOT)

            def head(i, first, last):
                for k in range(TOPK):
                    if k % BATCH == 0:
                        pe.wait_ge(dg["sem"], i * NB + at(dg, NB + k // BATCH + 1))
                    for c in range(2):
                        mm = pe.matmul(core["ps"][:, c, :], diag[:, k % (2 * BATCH), :],
                                       slots[:, k % NSLOT, D + c * 512:D + (c + 1) * 512],
                                       start=(first and k == 0), stop=(last and k == TOPK - 1))
                    mm.then_inc(free["sem"], 1)

            with pe.Fori(0, tiles) as t:
                pe.wait_ge(rd["sem"], t + at(rd, 1))
                head(t * PH, True, False)
                with pe.Fori(1, PH - 1) as hh:
                    head(t * PH + hh, False, False)
                head(t * PH + PH - 1, False, True)

        @block.scalar
        def _(act):
            def softmax(n):
                act.wait_ge(cho["sem"], n)
                act.activation(raised, shifted, ACT.Exp, accum_out=total[:, 0:1]).then_inc(exd["sem"], 1)

            act.sem_inc(dg["sem"], NB)
            softmax(at(cho, 18))
            with act.Fori(0, steps) as i:
                for b in range(NB):
                    s = slice(b * BATCH, (b + 1) * BATCH)
                    act.wait_ge(dot["sem"], i * TOPK + at(dot, (b + 1) * BATCH))
                    act.activation(gel[:, s], dots[:, s], ACT.Gelu).then_inc(gl["sem"], 1)
                    if b == 1:
                        softmax(i * CH + at(cho, CH + 18))
                    act.wait_ge(free["sem"], i * TOPK + at(free, NSLOT - BATCH + b * BATCH))
                    act.wait_ge(wt["sem"], i * NB + at(wt, b + 1))
                    for k in range(b * BATCH, (b + 1) * BATCH):
                        ins = act.activation(diag[:, k % (2 * BATCH), :], ident(core), ACT.Copy,
                                             scale=wts[:, k:k + 1])
                    ins.then_inc(dg["sem"], 1)

        @block.vector
        def _(dve):
            def choose(i, par, first, loaded):
                cur = ahead[:, 2 * par:2 * par + 2, :]
                dve.wait_ge(scl[par]["sem"], loaded)
                dve.sem_inc(ctn["sem"], 1)
                for s in range(2):
                    dve.max(best[:, s, 0:8], cur[:, s, :]).then_inc(cho["sem"], 1)
                dve.wait_ge(cho["sem"], first + 2)
                dve.sem_inc(ctn["sem"], 1)
                for s in range(2):
                    dve.max_index(where[:, s, 0:8], best[:, s, 0:8], cur[:, s, :]).then_inc(cho["sem"], 1)
                    dve.match_replace(cur2[:, s, :], best[:, s, 0:8], cur[:, s, :],
                                      LOWEST).then_inc(cho["sem"], 1)
                dve.wait_ge(cho["sem"], first + 6)
                dve.sem_inc(ctn["sem"], 1)
                for s in range(2):
                    dve.max(best[:, s, 8:16], cur2[:, s, :]).then_inc(cho["sem"], 1)
                dve.wait_ge(cho["sem"], first + 8)
                dve.sem_inc(ctn["sem"], 1)
                for s in range(2):
                    dve.max_index(where[:, s, 8:16], best[:, s, 8:16], cur2[:, s, :]).then_inc(cho["sem"], 1)
                dve.tensor_tensor(cand, bcast(best[:, 0, :], TOPK),
                                  best[:, 1:2, :].to_broadcast([P, TOPK, TOPK]), ALU.add).then_inc(cho["sem"], 1)
                dve.wait_ge(cho["sem"], first + 11)
                dve.sem_inc(ctn["sem"], 1)
                dve.max(score[:, 0:8], flat(cand)).then_inc(cho["sem"], 1)
                dve.tensor_copy(flat(wheref), flat(where)).then_inc(cho["sem"], 1)
                dve.wait_ge(cho["sem"], first + 13)
                dve.sem_inc(ctn["sem"], 1)
                dve.max_index(pick[:, 0:8], score[:, 0:8], flat(cand)).then_inc(cho["sem"], 1)
                dve.match_replace(flat(cand2), score[:, 0:8], flat(cand), LOWEST).then_inc(cho["sem"], 1)
                dve.wait_ge(cho["sem"], first + 15)
                dve.sem_inc(ctn["sem"], 1)
                dve.max(score[:, 8:16], flat(cand2)).then_inc(cho["sem"], 1)
                dve.wait_ge(cho["sem"], first + 16)
                dve.sem_inc(ctn["sem"], 1)
                dve.max_index(pick[:, 8:16], score[:, 8:16], flat(cand2)).then_inc(cho["sem"], 1)
                dve.tensor_scalar(shifted, score, score[:, 0:1], None, ALU.subtract).then_inc(cho["sem"], 1)
                dve.wait_ge(cho["sem"], first + 18)
                dve.tensor_scalar(halves[:, 0, :], pick, 4, None, ALU.logical_shift_right).then_inc(cho["sem"], 1)
                dve.tensor_scalar(halves[:, 1, :], pick, 15, None, ALU.bitwise_and).then_inc(cho["sem"], 1)
                dve.wait_ge(cho["sem"], first + 20)
                dve.tensor_copy(flat(halvesf), flat(halves)).then_inc(cho["sem"], 1)
                dve.wait_ge(cho["sem"], first + 21)
                dve.tensor_tensor(hot, bcast(flat(halvesf), TOPK),
                                  iota.unsqueeze(1).to_broadcast([P, 2 * TOPK, TOPK]),
                                  ALU.is_equal).then_inc(cho["sem"], 1)
                dve.wait_ge(cho["sem"], first + 22)
                hot4 = hot.rearrange("p (s k) j -> p s k j", s=2)
                dve.tensor_tensor(hot4, hot4, wheref.unsqueeze(2).to_broadcast([P, 2, TOPK, TOPK]),
                                  ALU.mult).then_inc(cho["sem"], 1)
                dve.wait_ge(cho["sem"], first + 23)
                dve.tensor_reduce(ef, hot, AX_X, ALU.add).then_inc(cho["sem"], 1)
                dve.wait_ge(exd["sem"], i + at(exd, 1))
                dve.reciprocal(total[:, 1:2], total[:, 0:1]).then_inc(cho["sem"], 1)
                dve.wait_ge(cho["sem"], first + 25)
                dve.tensor_scalar(gate[:, par, :], raised, total[:, 1:2], None, ALU.mult).then_inc(cho["sem"], 1)
                dve.scalar_tensor_tensor(out=expert[:, par, :], in0=ef[:, 0:TOPK], scalar=float(PK),
                                         in1=ef[:, TOPK:2 * TOPK], op0=ALU.mult,
                                         op1=ALU.add).then_inc(rdy["sem"], 1)

            def dot_batch(i, b):
                for k in range(b * BATCH, (b + 1) * BATCH):
                    s = k % NSLOT
                    dve.wait_ge(land[s]["sem"], i * 16 + at(land[s], 16))
                    u = slots[:, s, 0:D]
                    dve.tensor_tensor_reduce(u, u, h, 1.0, 0.0, ALU.mult, ALU.add,
                                             dots[:, k:k + 1]).then_inc(dot["sem"], 1)

            def weigh(i, par, b):
                s = slice(b * BATCH, (b + 1) * BATCH)
                dve.wait_ge(dg["sem"], i * NB + at(dg, b + 1))
                dve.wait_ge(gl["sem"], i * NB + at(gl, b + 1))
                dve.tensor_tensor(wts[:, s], gel[:, s], gate[:, par, s], ALU.mult).then_inc(wt["sem"], 1)

            dve.sem_inc(rd["sem"], 1)
            dve.sem_inc(hfree["sem"], 1)
            dve.wait_ge(g2l["sem"], at(g2l, 32))
            choose(0, 0, at(cho, 0), at(scl[0], 16))
            with dve.Fori(0, tiles) as t:
                with dve.Fori(0, PH // 2) as hh:
                    for par in range(2):
                        i = t * PH + hh * 2 + par
                        dve.wait_ge(hst["sem"], t * 16 + at(hst, 16))
                        dot_batch(i, 0)
                        dot_batch(i, 1)
                        dve.wait_ge(cho["sem"], i * CH + at(cho, CH))
                        weigh(i, par, 0)
                        choose(i + 1, 1 - par, i * CH + at(cho, CH),
                               (t * (PH // 2) + hh) * 16 + at(scl[1 - par], 16 + 16 * par))
                        weigh(i, par, 1)
                        dot_batch(i, 2)
                        dot_batch(i, 3)
                        weigh(i, par, 2)
                        weigh(i, par, 3)
                dve.wait_ge(free["sem"], t * PH * TOPK + at(free, NSLOT + PH * TOPK))
                dve.tensor_tensor(gated, pair(core, 0), g2[:, bass.ds((t // TL) * D, D)],
                                  ALU.mult).then_inc(rd["sem"], 1)
                dve.sem_inc(hfree["sem"], 1)
                dve.wait_ge(rd["sem"], t + at(rd, 2))
                xt = x[:, bass.ds(t * D, D)]
                dve.tensor_tensor(xt, xt, gated, ALU.add).then_inc(xup["sem"], 1)
                dve.wait_ge(xup["sem"], t + at(xup, 1))
    up(rdy, steps + 1)
    up(cho, (steps + 1) * CH)
    up(exd, steps + 1)
    up(hst, 16 * tiles)
    up(hfree, tiles + 1)
    for s in scl:
        up(s, 16 * (steps // 2 + 1))
    up(turn, steps * TOPK)
    up(ctn, 8 * (steps + 1))
    up(free, NSLOT + steps * TOPK)
    for s in land:
        up(s, 16 * steps)
    up(dot, steps * TOPK)
    up(gl, steps * NB)
    up(wt, steps * NB)
    up(dg, NB + steps * NB)
    up(rd, 1 + tiles)
    up(xup, tiles)
    close(core)


def store_stage(core, d):
    nc = core["nc"]
    st = signal(core, "output_stored")
    with nc.Block() as block:
        @block.sync
        def _(sp):
            sp.dma_start(d["out"].rearrange("(t p) n -> p t n", p=P),
                         view(core, XO, TL, D)).then_inc(st["sem"], up(st, 16))
            sp.wait_ge(st["sem"], at(st, 16))
    close(core)


def program(nc, d, stages):
    with ExitStack() as ctx:
        core = {"nc": nc, "ctx": ctx, "signals": {}, "gates": d["gates"],
                "h2_rows": d["h2_rows"], "score_rows": d["score_rows"],
                "sb": ctx.enter_context(nc.sbuf_tensor("arena", [P, WORDS], F32)),
                "ps": ctx.enter_context(nc.psum_tensor("banks", [P, 8, 512], F32))}
        core["ring"] = [signal(core, f"ring_slot{s}_loaded") for s in range(3)]
        load_constants(core, d)
        if "ada0" in stages:
            ada_stage(core, d, 0)
            ada_stage(core, d, 1)
        if "mix0" in stages:
            norm_stage(core, 0, 0, TT)
            project_stage(core, d)
            fourier_stage(core, d)
            ssd_stage(core, d)
            gate_stage(core, d)
            ft = view(core, FT_O, GROUPS, TOK)
            ms = view(core, BC_O, KD, TOK)
            col = lambda k, t: (ft[:, k, t * P:(t + 1) * P] if k < GROUPS
                                else ms[:, k - GROUPS, t * P:(t + 1) * P])
            out_stage(core, d["l0_w_out"], col, lambda c: view(core, RO + c * 6144, EVEN_OUT // P, 512),
                      XS_O, 0, TT)
        if "peer0" in stages:
            norm_stage(core, 0, 1, TT, view(core, H2_O, TT, D))
            peer_score_stage(core, d, 0, TT)
            peer_gather_stage(core, d, 0, TT)
        if "mix1" in stages:
            norm_stage(core, 1, 0, TT)
            mla_down_stage(core, d)
            mla_up_stage(core, d)
            attention_stage(core, d)
            ot = view(core, OT_O, KD, LAT)
            out_stage(core, d["l1_w_o"], lambda k, t: ot[:, k, t * P:(t + 1) * P],
                      lambda c: view(core, RO + (c + 1) * SLOT, KD, 512), KT_O, 1, TL)
        if "peer1" in stages:
            norm_stage(core, 1, 1, TL, view(core, H2_O, TT, D))
            peer_score_stage(core, d, 1, TL)
            peer_gather_stage(core, d, 1, TL)
        store_stage(core, d)


ALL = ("ada0", "mix0", "peer0", "mix1", "peer1")


def shape_constants():
    import numpy as np

    const = np.zeros((P, C_WORDS), np.float32)
    const[:, C_ID:C_ID + P] = np.eye(P)
    k, l = np.meshgrid(np.arange(P), np.arange(P), indexing="ij")
    const[:, C_TRI:C_TRI + P] = k <= l
    const[:, C_TRI + P:C_TRI + 2 * P] = k >= l
    const[:, C_NEG:C_NEG + P] = np.where(k > l, -1e30, 0)
    const[:, C_NEG + P:C_NEG + 2 * P] = np.where(k < l, -1e30, 0)
    const[:, C_ONE:C_ONE + P] = 1

    def dft(n, sign):
        a = 2 * np.pi * ((np.arange(n)[:, None] * np.arange(n)[None, :]) % n) / n
        return np.concatenate([np.cos(a), sign * np.sin(a)], 1) / np.sqrt(n)

    const[:, C_DFT:C_DFT + 2 * P] = dft(GDIM, 1.0)
    const[:, C_IOTA:C_IOTA + TOPK] = np.arange(TOPK)
    rows, cols = np.repeat(np.arange(LAT // 64), 64), np.arange(LAT) % 64
    inv = (np.float32(10000.0) ** (-np.arange(0, 16, 2, dtype=np.float32) / np.float32(16))).astype(np.float32)
    ang = np.concatenate([rows[:, None].astype(np.float32) * inv, cols[:, None].astype(np.float32) * inv], 1)
    rope = np.stack([np.cos(ang), np.sin(ang)], 0).astype(np.float32)
    rope = rope.reshape(2, TL, P, 16).transpose(2, 0, 1, 3).reshape(P, 2 * TL * 16)
    return {"const": const, "dft_lat": dft(LAT, -1.0).astype(np.float32),
            "dft_ctx": dft(CTX, -1.0).astype(np.float32), "rope": np.ascontiguousarray(rope)}


def kernel(**inputs):
    import numpy as np
    import concourse.bacc as bacc
    from concourse.bass_utils import run_bass_kernel_spmd

    a = {k: np.asarray(v) for k, v in inputs.items()}
    col = lambda v: v.reshape(-1, P).T
    arrays = dict(shape_constants())
    arrays["x"] = a["x"].reshape(LAT, D)
    arrays["ctx"] = a["ctx"].reshape(CTX, D)
    arrays["cond"] = np.stack([col(a["c"][0]), col(a["c_ctx"])], 2).reshape(P, 2 * KD)
    arrays["norms"] = np.concatenate([col(a[f"l{i}_norm{j}"]) for i in range(2) for j in (1, 2)], 1)
    for i in range(2):
        arrays[f"l{i}_w_ada"] = a[f"l{i}_w_ada"]
        arrays[f"l{i}_b_ada"] = a[f"l{i}_b_ada"].reshape(1, 6 * D)
        arrays[f"l{i}_peer_wq"] = a[f"l{i}_peer_wq"]
        arrays[f"keys{i}"] = a[f"l{i}_peer_keys"].transpose(3, 0, 1, 2).reshape(P, 2 * PH * PK)
        arrays[f"experts{i}"] = np.concatenate([a[f"l{i}_peer_u"], a[f"l{i}_peer_v"]], 1)
    arrays["l0_w_in"] = a["l0_w_in"]
    arrays["conv"] = np.concatenate([a["l0_conv_w"].reshape(TAPS, 16, P).transpose(2, 1, 0).reshape(P, 80),
                                     col(a["l0_conv_b"])], 1)
    arrays["ssd_rows"] = np.concatenate([a["l0_dt_bias"].reshape(1, 32), a["l0_a_log"].reshape(1, 32),
                                         a["l0_d_skip"].reshape(1, 32)], 1)
    arrays["ssd_norm"] = col(a["l0_ssd_norm"])
    arrays["l0_w_out"] = a["l0_w_out"]
    arrays["a_norms"] = np.concatenate([col(a["l1_q_a_norm"]), col(a["l1_kv_a_norm"])], 1)
    arrays["qk_norms"] = np.concatenate([a["l1_q_norm"], a["l1_k_norm"]]).reshape(1, 2 * QK)
    for n in ("l1_w_dqkv", "l1_w_uq", "l1_w_ukv", "l1_w_o"):
        arrays[n] = a[n]
    arrays = {k: np.ascontiguousarray(v) for k, v in arrays.items()}
    nc = bacc.Bacc("TRN2", target_bir_lowering=False, num_devices=1)
    d = {k: nc.dram_tensor(k, v.shape, F32, kind="ExternalInput").ap() for k, v in arrays.items()}
    d["gates"] = nc.dram_tensor("gates", (2, 2, 2, D), F32, kind="Internal").ap()
    d["h2_rows"] = nc.dram_tensor("h2_rows", (TT, P, D), F32, kind="Internal").ap()
    d["score_rows"] = nc.dram_tensor("score_rows", (TT * PH + 2, P, 2 * PK), F32, kind="Internal").ap()
    d["out"] = nc.dram_tensor("out", (LAT, D), F32, kind="ExternalOutput").ap()
    program(nc, d, ALL)
    r = run_bass_kernel_spmd(nc, [arrays], core_ids=[0])
    return r.results[0]["out"].reshape(1, LAT, D)
```

```python
from contextlib import ExitStack

import concourse.bass as bass
from concourse import mybir

F32 = mybir.dt.float32
BF16 = mybir.dt.bfloat16
U32 = mybir.dt.uint32
ALU = mybir.AluOpType
ACT = mybir.ActivationFunctionType
AX_X = mybir.AxisListType.X

P = 128
D = 1024
KD = D // P
LAT, CTX = 512, 256
TL, TC = LAT // P, CTX // P
TT = TL + TC
TOK = LAT + CTX
EPS = 1e-6

GROUPS, GDIM = 4, 128
FW = GROUPS * GDIM
HEADS, HD = 16, 64
INNER = HEADS * HD
SG, SN = 4, 128
HG = HEADS // SG
GW = HG * HD
TAPS = 5
CONV = INNER + 2 * SG * SN
EVEN_IN = FW + INNER + CONV + 2 * HEADS
EVEN_OUT = FW + INNER

MH, NOPE, ROPE, MV = 16, 64, 32, 64
QK = NOPE + ROPE
QL, KVL = 384, 256
ODD_IN = QL + KVL + ROPE

PH, PK, PQ, TOPK = 8, 128, 256, 16
EXPERTS = PK * PK
LOWEST = -3.0e38

C_ID, C_TRI, C_ONE, C_DFT, C_IOTA = 0, 128, 384, 512, 1024
C_WORDS = 1040
S_COND = 1040
S_MOD = 1056
S_NORM = S_MOD + 2 * 96
S_BIAS = S_NORM + 32
S_BF = S_BIAS + 96
S_BASE = S_BF + 192
XO = 2048
RO = XO + TT * D
SLOT = 4096
HO = RO + 3 * SLOT
L0 = HO + KD * TOK
MISC = L0 + 24576
WORDS = 53208



def up(sig, n=1):
    sig["total"] += n
    return n


def at(sig, n):
    return sig["base"] + n


def signal(core, name):
    if name not in core["signals"]:
        core["signals"][name] = {"sem": core["ctx"].enter_context(core["nc"].semaphore(name)),
                                 "base": 0, "total": 0}
    return core["signals"][name]


def close(core):
    for name in core["signals"]:
        core["signals"][name]["base"] = core["signals"][name]["total"]


def view(core, start, *shape):
    n = 1
    for s in shape:
        n *= s
    v = core["sb"][:, start:start + n]
    if len(shape) == 2:
        v = v.rearrange("p (a b) -> p a b", b=shape[1])
    if len(shape) == 3:
        v = v.rearrange("p (a b c) -> p a b c", b=shape[1], c=shape[2])
    return v


def pair(core, b):
    return core["ps"][:, b:b + 2, :].rearrange("p a b -> p (a b)")


def ident(core):
    return view(core, C_ID, P)


def ring_plan(core, chunks, slots=3):
    plan = []
    uses = [0] * slots
    for c in range(chunks):
        s = c % slots
        uses[s] += 1
        plan.append((s, core["ring"][s], at(core["ring"][s], 16 * uses[s])))
    return plan


def bcast(ap, n):
    return ap.unsqueeze(2).to_broadcast([ap.shape[0], ap.shape[1], n])


def load_constants(core, d):
    nc = core["nc"]
    loaded = signal(core, "constants_loaded")
    silu_done = signal(core, "cond_silu_done")
    cond = view(core, S_COND, KD, 2)
    with nc.Block() as block:
        @block.sync
        def _(sp):
            sp.dma_start(view(core, 0, C_WORDS), d["const"]).then_inc(loaded["sem"], up(loaded, 16))
            sp.dma_start(view(core, S_COND, KD * 2), d["cond"]).then_inc(loaded["sem"], up(loaded, 16))
            sp.dma_start(view(core, S_NORM, 4 * KD), d["norms"]).then_inc(loaded["sem"], up(loaded, 16))
            sp.dma_start(view(core, XO, TL, D),
                         d["x"].rearrange("(t p) n -> p t n", p=P)).then_inc(loaded["sem"], up(loaded, 16))
            sp.dma_start(view(core, XO + TL * D, TC, D),
                         d["ctx"].rearrange("(t p) n -> p t n", p=P)).then_inc(loaded["sem"], up(loaded, 16))
            sp.dma_start(view(core, S_BIAS, 12 * KD), d["ada_bias"]).then_inc(loaded["sem"], up(loaded, 16))
            sp.dma_start(view(core, S_BF, 192), d["const_bf"]).then_inc(loaded["sem"], up(loaded, 16))
            sp.wait_ge(loaded["sem"], at(loaded, 112))

        @block.scalar
        def _(act):
            act.wait_ge(loaded["sem"], at(loaded, 112))
            act.activation(cond, cond, ACT.Silu).then_inc(silu_done["sem"], up(silu_done))
    close(core)


def ada_tile(pe, core, wt, j, n, bank):
    cond = view(core, S_COND, KD, 2)
    for k in range(KD):
        i = pe.matmul(core["ps"][:, bank, 2 * n:2 * n + 2], wt[:, k, j * P:(j + 1) * P], cond[:, k, :],
                      start=(k == 0), stop=(k == KD - 1))
    return i


def ada_columns(dve, core, layer, bank, done):
    mod = view(core, S_MOD + layer * 96, 6 * KD, 2)
    bias = view(core, S_BIAS + layer * 6 * KD, 6 * KD)
    norms = view(core, S_NORM + layer * 2 * KD, 2, KD)
    dve.tensor_tensor(mod, core["ps"][:, bank, 0:12 * KD].rearrange("p (a b) -> p a b", b=2),
                      bcast(bias, 2), ALU.add).then_inc(done["sem"], up(done))
    dve.wait_ge(done["sem"], done["total"])
    for n, part in enumerate((1, 4)):
        c2 = mod[:, part * KD:(part + 1) * KD, :]
        dve.scalar_tensor_tensor(out=c2, in0=c2, scalar=1.0, in1=bcast(norms[:, n, :], 2),
                                 op0=ALU.add, op1=ALU.mult).then_inc(done["sem"], up(done))


def ada_turn_gates(pe, core, layer, bank, turned):
    mod = view(core, S_MOD + layer * 96, 6, 2 * KD)
    for n, part in enumerate((2, 5)):
        i = pe.transpose(core["ps"][0:2 * KD, bank, 128 + n * P:128 + (n + 1) * P], mod[:, part, :], ident(core))
    i.then_inc(turned["sem"], up(turned))


def gate_rows(core, layer, kind, cond):
    row = core["gates"][layer, kind].rearrange("(k c) n -> c k n", c=2)
    return row[cond:cond + 1].to_broadcast([P, KD, P])


def ada_stage(core, d):
    nc = core["nc"]
    N = 6 * D // 512
    plan = ring_plan(core, N)
    rows = view(core, MISC, 2, P)[0:2 * KD]
    cond = view(core, S_COND, KD, 2)
    row = view(core, HO, 6 * D)[0:2]
    mm = signal(core, "ada_product_done")
    ro = signal(core, "ada_rows_out")
    tc = signal(core, "ada_rows_turned")
    own = signal(core, "ada_columns_ready")
    tr = signal(core, "ada_gates_turned")
    cp = signal(core, "ada_gate_rows_out")
    st = signal(core, "gates_stored")
    w = d["l0_w_ada"].rearrange("(k p) n -> p k n", p=P)
    with nc.Block() as block:
        @block.sync
        def _(sp):
            for c, (s, sig, _v) in enumerate(plan):
                if c >= 3:
                    sp.wait_ge(mm["sem"], at(mm, c - 2))
                sp.dma_start(view(core, RO + s * SLOT, KD, 512),
                             w[:, :, c * 512:(c + 1) * 512]).then_inc(sig["sem"], up(sig, 16))
            sp.wait_ge(cp["sem"], at(cp, 1))
            for kind in range(2):
                sp.dma_start(core["gates"][0, kind], rows[:, kind, :]).then_inc(st["sem"], up(st, 16))
            sp.wait_ge(st["sem"], st["total"])

        @block.tensor
        def _(pe):
            for c, (s, sig, v) in enumerate(plan):
                pe.wait_ge(sig["sem"], v)
                if c >= 4:
                    pe.wait_ge(ro["sem"], at(ro, c - 3))
                wt = view(core, RO + s * SLOT, KD, 512)
                for k in range(KD):
                    i = pe.matmul(core["ps"][0:2, c % 4, :], cond[:, k, :], wt[:, k, :],
                                  start=(k == 0), stop=(k == KD - 1))
                i.then_inc(mm["sem"], up(mm))
            pe.wait_ge(ro["sem"], at(ro, N))
            for n in range(6 * KD):
                i = pe.transpose(core["ps"][:, 4, 2 * n:2 * n + 2], row[:, n * P:(n + 1) * P],
                                 ident(core)[0:2, 0:2])
            i.then_inc(tc["sem"], up(tc))
            pe.wait_ge(own["sem"], at(own, 1))
            ada_turn_gates(pe, core, 0, 1, tr)

        @block.vector
        def _(dve):
            for c in range(N):
                dve.wait_ge(mm["sem"], at(mm, c + 1))
                dve.tensor_copy(row[:, c * 512:(c + 1) * 512],
                                core["ps"][0:2, c % 4, :]).then_inc(ro["sem"], up(ro))
            dve.wait_ge(tc["sem"], at(tc, 1))
            ada_columns(dve, core, 0, 4, own)
            dve.wait_ge(tr["sem"], at(tr, 1))
            dve.tensor_copy(rows.rearrange("p a b -> p (a b)"),
                            core["ps"][0:2 * KD, 1, 128:128 + 2 * P]).then_inc(cp["sem"], up(cp))
    close(core)


def norm_stage(core, layer, which, tiles, h2=None):
    nc = core["nc"]
    x = view(core, XO, TT, D)
    ht = view(core, HO, KD, tiles * P)
    squares = view(core, RO, D)
    xn = view(core, RO + D, 2, D)
    ss = view(core, MISC, TT)
    rstd = view(core, MISC + 8, TT)
    mod = view(core, S_MOD + layer * 96, 6, 2 * KD)
    shift, scale = (mod[:, 3 * which + n, :].rearrange("p (k c) -> p k c", c=2) for n in range(2))
    sq = signal(core, "norm_squares_summed")
    root = signal(core, "norm_root_done")
    own = signal(core, "norm_rows_ready")
    tr = signal(core, "norm_rows_turned")
    cola = signal(core, "norm_low_columns_out")
    colv = signal(core, "norm_high_columns_out")
    back = signal(core, "norm_columns_turned_back")
    out = signal(core, "norm_h2_out")
    with nc.Block() as block:
        @block.scalar
        def _(act):
            for t in range(tiles):
                if t:
                    act.wait_ge(sq["sem"], sq["total"])
                act.activation(squares, x[:, t, :], ACT.Square,
                               accum_out=ss[:, t:t + 1]).then_inc(sq["sem"], up(sq))
            act.wait_ge(own["sem"], at(own, 1))
            act.activation(rstd[:, 0:tiles], ss[:, 0:tiles], ACT.Sqrt).then_inc(root["sem"], up(root))
            for t in range(tiles):
                c = 0 if t < TL else 1
                act.wait_ge(tr["sem"], at(tr, t + 1))
                for k in range(KD // 2):
                    i = act.activation(ht[:, k, t * P:(t + 1) * P],
                                       pair(core, 2 * (t % 2))[:, k * P:(k + 1) * P], ACT.Identity,
                                       bias=shift[:, k, c:c + 1], scale=scale[:, k, c:c + 1])
                i.then_inc(cola["sem"], up(cola))

        @block.vector
        def _(dve):
            dve.wait_ge(sq["sem"], at(sq, tiles))
            dve.tensor_scalar(ss[:, 0:tiles], ss[:, 0:tiles], 1.0 / D, EPS, ALU.mult,
                              ALU.add).then_inc(own["sem"], up(own))
            dve.wait_ge(root["sem"], at(root, 1))
            dve.reciprocal(rstd[:, 0:tiles], rstd[:, 0:tiles]).then_inc(own["sem"], up(own))
            dve.wait_ge(own["sem"], own["total"])
            for t in range(tiles + 2):
                if t < tiles:
                    if t >= 2:
                        dve.wait_ge(tr["sem"], at(tr, t - 1))
                    dve.tensor_scalar(xn[:, t % 2, :], x[:, t, :], rstd[:, t:t + 1], None,
                                      ALU.mult).then_inc(own["sem"], up(own))
                if 1 <= t <= tiles:
                    u = t - 1
                    c = 0 if u < TL else 1
                    dve.wait_ge(tr["sem"], at(tr, u + 1))
                    for k in range(KD // 2, KD):
                        i = dve.tensor_scalar(ht[:, k, u * P:(u + 1) * P],
                                              pair(core, 2 * (u % 2))[:, k * P:(k + 1) * P],
                                              scale[:, k, c:c + 1], shift[:, k, c:c + 1],
                                              ALU.mult, ALU.add)
                    i.then_inc(colv["sem"], up(colv))
                if t >= 2 and h2 is not None:
                    u = t - 2
                    dve.wait_ge(back["sem"], at(back, u + 1))
                    dve.tensor_copy(h2[:, u, :], pair(core, 4 + 2 * (u % 2))).then_inc(out["sem"], up(out))

        @block.tensor
        def _(pe):
            for t in range(tiles + 1):
                if t < tiles:
                    pe.wait_ge(own["sem"], at(own, t + 3))
                    if t >= 2:
                        pe.wait_ge(cola["sem"], at(cola, t - 1))
                        pe.wait_ge(colv["sem"], at(colv, t - 1))
                    for k in range(KD):
                        i = pe.transpose(pair(core, 2 * (t % 2))[:, k * P:(k + 1) * P],
                                         xn[:, t % 2, k * P:(k + 1) * P], ident(core))
                    i.then_inc(tr["sem"], up(tr))
                if t >= 1 and h2 is not None:
                    u = t - 1
                    pe.wait_ge(cola["sem"], at(cola, u + 1))
                    pe.wait_ge(colv["sem"], at(colv, u + 1))
                    if u >= 2:
                        pe.wait_ge(out["sem"], at(out, u - 1))
                    for k in range(KD):
                        i = pe.transpose(pair(core, 4 + 2 * (u % 2))[:, k * P:(k + 1) * P],
                                         ht[:, k, u * P:(u + 1) * P], ident(core))
                    i.then_inc(back["sem"], up(back))
    close(core)


FT_O = L0
ZS_O = FT_O + GROUPS * TOK
BC_O = ZS_O + TT * INNER
XS_O = BC_O + 2 * SG * TOK
BR_O = XS_O + TT * INNER
SEG = 2 + LAT + 2 + 2 + CTX + 2
CO = LAT + 4
S_CW = S_BASE
S_DTR = S_BASE + 96


def project_stage(core, d):
    nc = core["nc"]
    ht = view(core, HO, KD, TOK)
    ft = view(core, FT_O, GROUPS, TOK)
    zs = view(core, ZS_O, TT, INNER)
    bct = view(core, BC_O, 2 * SG, TOK)
    xs = view(core, XS_O, TT, INNER)
    br = view(core, BR_O, TT, SG * SN)
    cw = view(core, S_CW, 16, TAPS)
    cb = view(core, S_CW + 80, 16)
    dtr = view(core, S_DTR, TT, 2 * HEADS)
    pad = [view(core, RO + 2 * SLOT, SEG), view(core, RO + 2 * SLOT + SEG, SEG)]
    acc = [view(core, RO + 2 * SLOT + 2 * SEG, SEG), view(core, RO + 2 * SLOT + 3 * SEG, SEG)]
    sil = [view(core, MISC, TOK), view(core, MISC + TOK, TOK)]
    w = d["l0_w_in"].rearrange("(k p) n -> p k n", p=P)
    UT = (FW + CONV) // P
    starts = [0] + [FW + INNER + 512 * c for c in range(4)] + [FW, FW + 512, EVEN_IN - 2 * HEADS]
    widths = [512] * 7 + [2 * HEADS]
    plan = ring_plan(core, 8, 2)
    taps_in = signal(core, "conv_taps_loaded")
    zero = signal(core, "conv_pads_zeroed")
    mm = signal(core, "project_product_done")
    ev = signal(core, "project_banks_read")
    cv = signal(core, "conv_step")
    si = signal(core, "conv_silu_done")
    tr = signal(core, "conv_columns_turned")
    rw = signal(core, "conv_rows_out")
    NF, NU = GROUPS, UT
    NR = 12

    with nc.Block() as block:
        @block.sync
        def _(sp):
            sp.dma_start(view(core, S_CW, 96), d["conv"]).then_inc(taps_in["sem"], up(taps_in, 16))
            for c, (s, sig, _v) in enumerate(plan):
                if c >= 2:
                    q = c - 2
                    n = 4 * (q + 1) if q < 5 else NU + 6 * (q - 4)
                    sp.wait_ge(mm["sem"], at(mm, n))
                sp.dma_start(view(core, RO + s * SLOT, KD, 512)[:, :, 0:widths[c]],
                             w[:, :, starts[c]:starts[c] + widths[c]]).then_inc(sig["sem"], up(sig, 16))

        @block.gpsimd
        def _(pool):
            for b in range(2):
                pool.memset(pad[b], 0.0).then_inc(zero["sem"], up(zero))

        @block.tensor
        def _(pe):
            def turn(u):
                v = u - NF
                pe.wait_ge(si["sem"], at(si, v + 1))
                if v >= 2:
                    pe.wait_ge(rw["sem"], at(rw, v - 1))
                for t in range(TT):
                    i = pe.transpose(pair(core, 4 + 2 * (v % 2))[:, t * P:(t + 1) * P],
                                     sil[v % 2][:, t * P:(t + 1) * P] if v < 8 else
                                     bct[:, v - 8, t * P:(t + 1) * P], ident(core))
                i.then_inc(tr["sem"], up(tr))

            for u in range(NU):
                s, sig, v = plan[u // 4]
                if u % 4 == 0:
                    pe.wait_ge(sig["sem"], v)
                if u >= 2:
                    pe.wait_ge(ev["sem"], at(ev, u - 1))
                wt = view(core, RO + s * SLOT, KD, 512)
                o = pair(core, 2 * (u % 2))
                for a, b in ((0, LAT), (LAT, TOK)):
                    for k in range(KD):
                        i = pe.matmul(o[:, a:b], wt[:, k, (u % 4) * P:(u % 4 + 1) * P], ht[:, k, a:b],
                                      start=(k == 0), stop=(k == KD - 1))
                i.then_inc(mm["sem"], up(mm))
                if NF <= u - 2 < NF + NR:
                    turn(u - 2)
            n = 0
            for c in range(5, 8):
                s, sig, v = plan[c]
                pe.wait_ge(sig["sem"], v)
                wt = view(core, RO + s * SLOT, KD, 512)
                for t in range(TT):
                    pe.wait_ge(ev["sem"], at(ev, NU + n - 3 if n >= 4 else NU))
                    for k in range(KD):
                        i = pe.matmul(core["ps"][:, n % 4, 0:widths[c]], ht[:, k, t * P:(t + 1) * P],
                                      wt[:, k, 0:widths[c]], start=(k == 0), stop=(k == KD - 1))
                    i.then_inc(mm["sem"], up(mm))
                    n += 1

        @block.scalar
        def _(act):
            def silu(u):
                v = u - NF
                act.wait_ge(cv["sem"], at(cv, TAPS * (v + 1)))
                if v < 8:
                    if v >= 2:
                        act.wait_ge(tr["sem"], at(tr, v - 1))
                    o = sil[v % 2]
                else:
                    o = bct[:, v - 8, :]
                act.activation(o[:, 0:LAT], acc[v % 2][:, 0:LAT], ACT.Silu)
                act.activation(o[:, LAT:TOK], acc[v % 2][:, CO:CO + CTX],
                               ACT.Silu).then_inc(si["sem"], up(si))

            act.wait_ge(zero["sem"], at(zero, 2))
            for u in range(NU):
                act.wait_ge(mm["sem"], at(mm, u + 1))
                o = pair(core, 2 * (u % 2))
                if u < NF:
                    act.activation(ft[:, u, :], o[:, 0:TOK], ACT.Copy).then_inc(ev["sem"], up(ev))
                    continue
                v = u - NF
                if v >= 2:
                    act.wait_ge(cv["sem"], at(cv, TAPS * (v - 1)))
                act.activation(pad[v % 2][:, 2:2 + LAT], o[:, 0:LAT], ACT.Copy)
                act.activation(pad[v % 2][:, CO + 2:CO + 2 + CTX], o[:, LAT:TOK],
                               ACT.Copy).then_inc(ev["sem"], up(ev))
                if v >= 1:
                    silu(u - 1)
            silu(NU - 1)
            for n in range(3 * TT):
                act.wait_ge(mm["sem"], at(mm, NU + n + 1))
                t = n % TT
                if n < 2 * TT:
                    c = n // TT
                    act.activation(zs[:, t, c * 512:(c + 1) * 512], core["ps"][:, n % 4, :],
                                   ACT.Silu).then_inc(ev["sem"], up(ev))
                else:
                    act.activation(dtr[:, t, :], core["ps"][:, n % 4, 0:2 * HEADS],
                                   ACT.Copy).then_inc(ev["sem"], up(ev))

        @block.vector
        def _(dve):
            W = SEG - 4
            def rows(v):
                dve.wait_ge(tr["sem"], at(tr, v + 1))
                o = (xs[:, :, v * P:(v + 1) * P] if v < 8 else br[:, :, (v - 8) * P:(v - 7) * P])
                dve.tensor_copy(o, pair(core, 4 + 2 * (v % 2))[:, 0:TOK].rearrange(
                    "p (t n) -> p t n", n=P)).then_inc(rw["sem"], up(rw))

            dve.wait_ge(taps_in["sem"], at(taps_in, 16))
            for v in range(NU - NF):
                dve.wait_ge(ev["sem"], at(ev, NF + v + 1))
                if v >= 2:
                    dve.wait_ge(si["sem"], at(si, v - 1))
                a = acc[v % 2]
                dve.tensor_scalar(a[:, 0:W], pad[v % 2][:, 0:W], cw[:, v, 0:1], cb[:, v:v + 1],
                                  ALU.mult, ALU.add).then_inc(cv["sem"], up(cv))
                for j in range(1, TAPS):
                    dve.wait_ge(cv["sem"], cv["total"])
                    dve.scalar_tensor_tensor(out=a[:, 0:W], in0=pad[v % 2][:, j:j + W],
                                             scalar=cw[:, v, j:j + 1], in1=a[:, 0:W],
                                             op0=ALU.mult, op1=ALU.add).then_inc(cv["sem"], up(cv))
                if 2 <= v < NR + 2:
                    rows(v - 2)
    close(core)


def fourier_stage(core, d):
    nc = core["nc"]
    ft = view(core, FT_O, GROUPS, TOK)
    uv = view(core, RO, TT, GROUPS * 2 * GDIM)[:, :, :]
    cl = view(core, RO + 6144, TL, 2 * LAT)
    cc = view(core, RO + 6144 + TL * 2 * LAT, TC, 2 * CTX)
    dft = view(core, C_DFT, 2 * GDIM)
    tab = signal(core, "dft_tables_loaded")
    mm = signal(core, "dft_channels_done")
    ev = signal(core, "dft_channels_out")
    pm = signal(core, "dft_positions_done")
    po = signal(core, "dft_positions_out")
    N = TT * 2
    with nc.Block() as block:
        @block.sync
        def _(sp):
            sp.dma_start(cl, d["dft_lat"].rearrange("(t p) n -> p t n", p=P)).then_inc(tab["sem"], up(tab, 16))
            sp.dma_start(cc, d["dft_ctx"].rearrange("(t p) n -> p t n", p=P)).then_inc(tab["sem"], up(tab, 16))

        @block.tensor
        def _(pe):
            for n in range(N):
                if n >= 4:
                    pe.wait_ge(ev["sem"], at(ev, n - 3))
                t = n // 2
                for j in range(2):
                    i = pe.matmul(core["ps"][:, n % 4, j * 256:(j + 1) * 256],
                                  ft[:, 2 * (n % 2) + j, t * P:(t + 1) * P], dft, start=True, stop=True)
                i.then_inc(mm["sem"], up(mm))
            pe.wait_ge(tab["sem"], at(tab, 32))
            pe.wait_ge(ev["sem"], at(ev, N))
            for n in range(2 * GROUPS):
                g = n // 2
                tiles, first, tb, L = ((TL, 0, cl, LAT), (TC, TL, cc, CTX))[n % 2]
                if n >= 4:
                    pe.wait_ge(po["sem"], at(po, n - 3))
                for t in range(tiles):
                    for part in range(2):
                        i = pe.matmul(core["ps"][:, 4 + n % 4, 0:L],
                                      uv[:, first + t, g * 256 + part * P:g * 256 + (part + 1) * P],
                                      tb[:, t, part * L:(part + 1) * L],
                                      start=(t == 0 and part == 0), stop=(t == tiles - 1 and part == 1))
                i.then_inc(pm["sem"], up(pm))

        @block.vector
        def _(dve):
            for n in range(N):
                dve.wait_ge(mm["sem"], at(mm, n + 1))
                dve.tensor_copy(uv[:, n // 2, (n % 2) * 512:(n % 2 + 1) * 512],
                                core["ps"][:, n % 4, :]).then_inc(ev["sem"], up(ev))
            for n in range(2 * GROUPS):
                dve.wait_ge(pm["sem"], at(pm, n + 1))
                a, L = ((0, LAT), (LAT, CTX))[n % 2]
                dve.tensor_copy(ft[:, n // 2, a:a + L], core["ps"][:, 4 + n % 4, 0:L]).then_inc(po["sem"], up(po))
    close(core)


def ssd_stage(core, d):
    nc = core["nc"]
    y = view(core, HO, TT, INNER)
    bct = view(core, BC_O, 2 * SG, TOK)
    xs = view(core, XS_O, TT, INNER)
    br = view(core, BR_O, TT, SG * SN)
    dtr = view(core, S_DTR, TT, 2 * HEADS)
    E = view(core, RO, 2, 512)
    M = view(core, RO + 1024, 2, 512)
    XD = view(core, RO + 2048, 2, GW)
    XE = view(core, RO + 2560, 2, GW)
    TMP = view(core, RO + 3072, GW)
    HS = view(core, RO + 3328, 2, INNER)
    rows = view(core, RO + 5376, 5, 32)
    W = TT * 2 * HEADS
    DT, DTA, ACS, EAC, NAC, TOE, CD, T0, T1 = (view(core, RO + 5536 + i * W, TT, 2 * HEADS) for i in range(9))
    flat = lambda v: v.rearrange("p a b -> p (a b)")
    tri = view(core, C_TRI, 2, P)
    neg = view(core, S_BF + 64, P).bitcast(BF16).rearrange("p (r l) -> p r l", l=P)
    ident_bf = view(core, S_BF, 64).bitcast(BF16)
    ones = view(core, C_ONE, P)
    ld = signal(core, "ssd_rows_loaded")
    ex = signal(core, "ssd_prepare_act")
    pr = signal(core, "ssd_prepare_dve")
    sm = signal(core, "ssd_sums_done")
    fr = signal(core, "ssd_scores_done")
    eo = signal(core, "ssd_decay_ready")
    mo = signal(core, "ssd_masked_ready")
    xo = signal(core, "ssd_inputs_ready")
    bk = signal(core, "ssd_products_done")
    ac = signal(core, "ssd_added")
    order = [[4, 5, 0, 1, 2, 3], [5, 4, 3, 2, 1, 0]]
    steps = [(r, t, g) for r in range(2) for t in order[r] for g in range(SG)]
    NS = len(steps)
    assert NS == 6 * KD
    plan = ring_plan(core, NS // 2, 2)
    ada_w = [view(core, RO + 2 * SLOT + s * 2048, KD, 256) for s in range(2)]
    gate_out = view(core, MISC, 2, P)[0:2 * KD]
    w_ada = d["l1_w_ada"].rearrange("(k p) n -> p k n", p=P)
    am = signal(core, "ada_product_done")
    ao = signal(core, "ada_columns_ready")
    atr = signal(core, "ada_gates_turned")
    ago = signal(core, "ada_gate_rows_out")
    st = signal(core, "gates_stored")
    with nc.Block() as block:
        @block.sync
        def _(sp):
            sp.dma_start(flat(rows[:, 0:3, :]), d["ssd_rows"].to_broadcast([P, 96])).then_inc(ld["sem"], up(ld, 16))
            for c, (s, sig, _v) in enumerate(plan):
                if c >= 2:
                    sp.wait_ge(am["sem"], at(am, c - 1))
                sp.dma_start(ada_w[s], w_ada[:, :, c * 256:(c + 1) * 256]).then_inc(sig["sem"], up(sig, 16))
            sp.wait_ge(ago["sem"], at(ago, 1))
            for kind in range(2):
                sp.dma_start(core["gates"][1, kind], gate_out[:, kind, :]).then_inc(st["sem"], up(st, 16))
            sp.wait_ge(st["sem"], st["total"])

        @block.scalar
        def _(act):
            act.wait_ge(ld["sem"], at(ld, 16))
            act.activation(rows[:, 3, :], rows[:, 1, :], ACT.Exp).then_inc(ex["sem"], up(ex))
            act.wait_ge(pr["sem"], at(pr, 2))
            act.activation(flat(T1), flat(T1), ACT.Exp).then_inc(ex["sem"], up(ex))
            act.wait_ge(ex["sem"], ex["total"])
            act.activation(flat(T1), flat(T1), ACT.Ln, bias=1.0).then_inc(ex["sem"], up(ex))
            act.wait_ge(pr["sem"], at(pr, 8))
            act.activation(flat(EAC), flat(ACS), ACT.Exp).then_inc(ex["sem"], up(ex))
            act.activation(flat(TOE), flat(TOE), ACT.Exp).then_inc(ex["sem"], up(ex))
            act.activation(flat(CD), flat(CD), ACT.Exp).then_inc(ex["sem"], up(ex))
            for n, (r, t, g) in enumerate(steps):
                act.wait_ge(fr["sem"], at(fr, n + 1))
                if n >= 2:
                    act.wait_ge(mo["sem"], at(mo, n - 1))
                for h in range(HG):
                    c = r * HEADS + g * HG + h
                    i = act.activation(E[:, n % 2, h * P:(h + 1) * P], core["ps"][:, n % 2, h * P:(h + 1) * P],
                                       ACT.Exp, bias=NAC[:, t, c:c + 1])
                i.then_inc(eo["sem"], up(eo))

        @block.vector
        def _(dve):
            dve.wait_ge(ld["sem"], at(ld, 16))
            dve.tensor_tensor(T0, dtr, rows[:, 0:1, :].to_broadcast([P, TT, 32]),
                              ALU.add).then_inc(pr["sem"], up(pr))
            dve.wait_ge(pr["sem"], pr["total"])
            dve.scalar_tensor_tensor(out=flat(T1), in0=flat(T0), scalar=-1.0, in1=flat(T0),
                                     op0=ALU.mult, op1=ALU.min).then_inc(pr["sem"], up(pr))
            dve.wait_ge(ex["sem"], at(ex, 3))
            dve.scalar_tensor_tensor(out=flat(DT), in0=flat(T0), scalar=0.0, in1=flat(T1),
                                     op0=ALU.max, op1=ALU.add).then_inc(pr["sem"], up(pr))
            dve.wait_ge(pr["sem"], pr["total"])
            dve.scalar_tensor_tensor(out=DTA, in0=DT, scalar=-1.0,
                                     in1=rows[:, 3:4, :].to_broadcast([P, TT, 32]),
                                     op0=ALU.mult, op1=ALU.mult).then_inc(pr["sem"], up(pr))
            dve.wait_ge(sm["sem"], at(sm, 1))
            for r in range(2):
                i = dve.tensor_copy(ACS[:, :, r * HEADS:(r + 1) * HEADS],
                                    core["ps"][:, r, 0:W].rearrange("p (a b) -> p a b", b=32)
                                    [:, :, r * HEADS:(r + 1) * HEADS])
            i.then_inc(pr["sem"], up(pr))
            dve.tensor_copy(flat(CD), core["ps"][:, 2, 0:W]).then_inc(pr["sem"], up(pr))
            dve.wait_ge(pr["sem"], pr["total"])
            dve.tensor_tensor(flat(TOE), flat(CD), flat(ACS), ALU.subtract).then_inc(pr["sem"], up(pr))
            dve.tensor_scalar(flat(NAC), flat(ACS), -1.0, None, ALU.mult).then_inc(pr["sem"], up(pr))
            dve.tensor_tensor(rows[:, 4, 0:16], rows[:, 2, 0:16], rows[:, 2, 16:32],
                              ALU.add).then_inc(pr["sem"], up(pr))
            dve.memset(flat(HS), 0.0).then_inc(pr["sem"], up(pr))
            dve.wait_ge(pr["sem"], pr["total"])
            for t in range(TT):
                dve.tensor_tensor(y[:, t, :].rearrange("p (h c) -> p h c", c=HD),
                                  xs[:, t, :].rearrange("p (h c) -> p h c", c=HD),
                                  bcast(rows[:, 4, 0:16], HD), ALU.mult).then_inc(pr["sem"], up(pr))
            dve.wait_ge(ex["sem"], at(ex, 6))

            def mask(n):
                dve.wait_ge(eo["sem"], at(eo, n + 1))
                dve.wait_ge(fr["sem"], at(fr, n + 1))
                if n >= 2:
                    dve.wait_ge(bk["sem"], at(bk, n - 1))
                sc = core["ps"][:, 2 + n % 2, 0:P].unsqueeze(1).to_broadcast([P, HG, P])
                dve.tensor_tensor(M[:, n % 2, :].rearrange("p (h l) -> p h l", l=P),
                                  E[:, n % 2, :].rearrange("p (h l) -> p h l", l=P), sc,
                                  ALU.mult).then_inc(mo["sem"], up(mo))

            def add(n):
                r, t, g = steps[n]
                c = r * HEADS + g * HG
                yg = y[:, t, g * GW:(g + 1) * GW]
                hs = HS[:, r, g * GW:(g + 1) * GW]
                per = lambda v: v.rearrange("p (h c) -> p h c", c=HD)
                dve.wait_ge(bk["sem"], at(bk, n + 1))
                if n:
                    dve.wait_ge(ac["sem"], ac["total"])
                dve.tensor_tensor(per(TMP), per(core["ps"][:, 4 + n % 2, GW:2 * GW]),
                                  bcast(EAC[:, t, c:c + HG], HD), ALU.mult).then_inc(ac["sem"], up(ac))
                dve.tensor_tensor(yg, yg, core["ps"][:, 4 + n % 2, 0:GW], ALU.add).then_inc(ac["sem"], up(ac))
                dve.tensor_tensor(per(hs), per(hs), bcast(CD[:, t, c:c + HG], HD),
                                  ALU.mult).then_inc(ac["sem"], up(ac))
                dve.wait_ge(ac["sem"], ac["total"])
                dve.tensor_tensor(yg, yg, TMP, ALU.add).then_inc(ac["sem"], up(ac))
                dve.tensor_tensor(hs, hs, core["ps"][:, 6, 0:GW], ALU.add).then_inc(ac["sem"], up(ac))

            dve.wait_ge(pr["sem"], pr["total"])
            mask(0)
            for n in range(NS):
                if n + 1 < NS:
                    mask(n + 1)
                add(n)
            dve.wait_ge(am["sem"], at(am, NS // 2))
            ada_columns(dve, core, 1, 7, ao)
            dve.wait_ge(atr["sem"], at(atr, 1))
            dve.tensor_copy(gate_out.rearrange("p a b -> p (a b)"),
                            core["ps"][0:2 * KD, 0, 128:128 + 2 * P]).then_inc(ago["sem"], up(ago))

        @block.gpsimd
        def _(pool):
            pool.wait_ge(pr["sem"], at(pr, 3))
            pool.wait_ge(ex["sem"], at(ex, 6))
            for n, (r, t, g) in enumerate(steps):
                c = r * HEADS + g * HG
                per = lambda v: v.rearrange("p (h c) -> p h c", c=HD)
                if n >= 2:
                    pool.wait_ge(bk["sem"], at(bk, n - 1))
                pool.tensor_tensor(per(XD[:, n % 2, :]), per(xs[:, t, g * GW:(g + 1) * GW]),
                                   bcast(DT[:, t, c:c + HG], HD), ALU.mult).then_inc(xo["sem"], up(xo))
                pool.wait_ge(xo["sem"], xo["total"])
                pool.tensor_tensor(per(XE[:, n % 2, :]), per(XD[:, n % 2, :]),
                                   bcast(TOE[:, t, c:c + HG], HD), ALU.mult).then_inc(xo["sem"], up(xo))

        @block.tensor
        def _(pe):
            pe.wait_ge(pr["sem"], at(pr, 4))
            for b, m in enumerate((tri[:, 0, :], tri[:, 1, :], ones)):
                i = pe.matmul(core["ps"][:, b, 0:W], m, flat(DTA), start=True, stop=True)
            i.then_inc(sm["sem"], up(sm))
            pe.wait_ge(pr["sem"], at(pr, 6))

            def front(n):
                r, t, g = steps[n]
                if n >= 2:
                    pe.wait_ge(eo["sem"], at(eo, n - 1))
                    pe.wait_ge(mo["sem"], at(mo, n - 1))
                pe.matmul(core["ps"][:, 2 + n % 2, 0:P], bct[:, g, t * P:(t + 1) * P],
                          bct[:, SG + g, t * P:(t + 1) * P], start=True, stop=True)
                pe.matmul(core["ps"][:, n % 2, :].rearrange("p (h l) -> p h l", l=P), ident_bf,
                          neg[:, r:r + 1, :].to_broadcast([P, HG, P]), start=True, stop=False)
                for h in range(HG):
                    c = r * HEADS + g * HG + h
                    i = pe.matmul(core["ps"][:, n % 2, h * P:(h + 1) * P],
                                  DTA[:, t, c:c + 1].to_broadcast([P, P]), tri[:, r, :],
                                  start=False, stop=(h == HG - 1))
                i.then_inc(fr["sem"], up(fr))

            front(0)
            for n, (r, t, g) in enumerate(steps):
                if n + 1 < NS:
                    front(n + 1)
                pe.wait_ge(mo["sem"], at(mo, n + 1))
                pe.wait_ge(xo["sem"], at(xo, 2 * n + 2))
                if n >= 4:
                    pe.wait_ge(ac["sem"], at(ac, 5 * (n - 3)))
                else:
                    pe.wait_ge(pr["sem"], at(pr, 10))
                    if n >= 2:
                        pe.wait_ge(ac["sem"], at(ac, 5 * (n - 1)))
                if n >= 4:
                    pe.wait_ge(ac["sem"], at(ac, 5 * (n - 1)))
                for h in range(HG):
                    pe.matmul(core["ps"][:, 4 + n % 2, h * HD:(h + 1) * HD], M[:, n % 2, h * P:(h + 1) * P],
                              XD[:, n % 2, h * HD:(h + 1) * HD], start=True, stop=True)
                pe.matmul(core["ps"][:, 4 + n % 2, GW:2 * GW], bct[:, SG + g, t * P:(t + 1) * P],
                          HS[:, r, g * GW:(g + 1) * GW], start=True, stop=True)
                if n:
                    pe.wait_ge(ac["sem"], at(ac, 5 * n))
                pe.matmul(core["ps"][:, 6, 0:GW], br[:, t, g * SN:(g + 1) * SN], XE[:, n % 2, :],
                          start=True, stop=True).then_inc(bk["sem"], up(bk))
                s, sig, v = plan[n // 2]
                if n % 2 == 0:
                    pe.wait_ge(sig["sem"], v)
                i = ada_tile(pe, core, ada_w[s], n % 2, n, 7)
                if n % 2:
                    i.then_inc(am["sem"], up(am))
            pe.wait_ge(ao["sem"], at(ao, 1))
            ada_turn_gates(pe, core, 1, 0, atr)
    close(core)


def gate_stage(core, d):
    nc = core["nc"]
    y = view(core, HO, TT, INNER)
    zs = view(core, ZS_O, TT, INNER)
    ms = view(core, BC_O, KD, TOK)
    sq = view(core, RO, INNER)
    ss = view(core, S_BASE, TT * SG)
    rstd = view(core, S_BASE + 32, TT * SG)
    gain = view(core, S_BASE + 64, KD)
    ld = signal(core, "ssd_gain_loaded")
    gt = signal(core, "gate_rows_step")
    qs = signal(core, "gate_squares_summed")
    tr = signal(core, "gate_rows_turned")
    ca = signal(core, "gate_low_columns_out")
    cv = signal(core, "gate_high_columns_out")
    with nc.Block() as block:
        @block.sync
        def _(sp):
            sp.dma_start(gain, d["ssd_norm"]).then_inc(ld["sem"], up(ld, 16))

        @block.vector
        def _(dve):
            for t in range(TT):
                dve.tensor_tensor(y[:, t, :], y[:, t, :], zs[:, t, :], ALU.mult).then_inc(gt["sem"], up(gt))
            dve.wait_ge(qs["sem"], at(qs, TT))
            dve.tensor_scalar(ss, ss, 1.0 / GW, EPS, ALU.mult, ALU.add).then_inc(gt["sem"], up(gt))
            dve.wait_ge(qs["sem"], at(qs, TT + 1))
            dve.reciprocal(rstd, rstd).then_inc(gt["sem"], up(gt))
            dve.wait_ge(gt["sem"], gt["total"])
            dve.wait_ge(ld["sem"], at(ld, 16))
            for t in range(TT + 1):
                if t < TT:
                    yt = y[:, t, :].rearrange("p (g c) -> p g c", c=GW)
                    dve.tensor_tensor(yt, yt, bcast(rstd[:, t * SG:(t + 1) * SG], GW),
                                      ALU.mult).then_inc(gt["sem"], up(gt))
                if t >= 1:
                    u = t - 1
                    dve.wait_ge(tr["sem"], at(tr, u + 1))
                    for k in range(KD // 2, KD):
                        i = dve.tensor_scalar(ms[:, k, u * P:(u + 1) * P],
                                              pair(core, 2 * (u % 2))[:, k * P:(k + 1) * P],
                                              gain[:, k:k + 1], None, ALU.mult)
                    i.then_inc(cv["sem"], up(cv))

        @block.scalar
        def _(act):
            for t in range(TT):
                act.wait_ge(gt["sem"], at(gt, t + 1))
                if t:
                    act.wait_ge(qs["sem"], qs["total"])
                for g in range(SG):
                    i = act.activation(sq[:, g * GW:(g + 1) * GW], y[:, t, g * GW:(g + 1) * GW], ACT.Square,
                                       accum_out=ss[:, t * SG + g:t * SG + g + 1])
                i.then_inc(qs["sem"], up(qs))
            act.wait_ge(gt["sem"], at(gt, TT + 1))
            act.activation(rstd, ss, ACT.Sqrt).then_inc(qs["sem"], up(qs))
            act.wait_ge(ld["sem"], at(ld, 16))
            for t in range(TT):
                act.wait_ge(tr["sem"], at(tr, t + 1))
                for k in range(KD // 2):
                    i = act.activation(ms[:, k, t * P:(t + 1) * P],
                                       pair(core, 2 * (t % 2))[:, k * P:(k + 1) * P], ACT.Copy,
                                       scale=gain[:, k:k + 1])
                i.then_inc(ca["sem"], up(ca))

        @block.tensor
        def _(pe):
            for t in range(TT):
                pe.wait_ge(gt["sem"], at(gt, TT + 3 + t))
                if t >= 2:
                    pe.wait_ge(ca["sem"], at(ca, t - 1))
                    pe.wait_ge(cv["sem"], at(cv, t - 1))
                for k in range(KD):
                    i = pe.transpose(pair(core, 2 * (t % 2))[:, k * P:(k + 1) * P],
                                     y[:, t, k * P:(k + 1) * P], ident(core))
                i.then_inc(tr["sem"], up(tr))
    close(core)


def out_stage(core, weights, lhs, wcols, gates, layer, tiles):
    nc = core["nc"]
    K = weights.shape[0] // P
    x = view(core, XO, TT, D)
    w = weights.rearrange("(k p) n -> p k n", p=P)
    gr = view(core, gates, 2, D)
    prod = view(core, MISC, 2, 512)
    ld = [signal(core, f"out_weights{c}_loaded") for c in range(4)]
    gl = signal(core, "out_gates_loaded")
    mm = signal(core, "out_product_done")
    gd = signal(core, "out_gated")
    ad = signal(core, "out_added")
    with nc.Block() as block:
        @block.sync
        def _(sp):
            half = K // 2
            for c in range(2):
                for part, (a, b) in enumerate(((0, half), (half, K))):
                    sig = ld[2 * c + part]
                    sp.dma_start(wcols(c)[:, a:b, :],
                                 w[:, a:b, c * 512:(c + 1) * 512]).then_inc(sig["sem"], up(sig, 16))
            for n in range(2):
                sp.dma_start(gr[:, n, :].rearrange("p (k l) -> p k l", l=P), gate_rows(core, layer, 0, n)
                             ).then_inc(gl["sem"], up(gl, 16))

        @block.tensor
        def _(pe):
            n = 0
            for c in range(2):
                pe.wait_ge(ld[2 * c]["sem"], at(ld[2 * c], 16))
                for t in range(tiles):
                    if n >= 4:
                        pe.wait_ge(gd["sem"], at(gd, n - 3))
                    for k in range(K):
                        if t == 0 and k == K // 2:
                            pe.wait_ge(ld[2 * c + 1]["sem"], at(ld[2 * c + 1], 16))
                        i = pe.matmul(core["ps"][:, n % 4, :], lhs(k, t), wcols(c)[:, k, :],
                                      start=(k == 0), stop=(k == K - 1))
                    i.then_inc(mm["sem"], up(mm))
                    n += 1

        @block.vector
        def _(dve):
            dve.wait_ge(gl["sem"], at(gl, 32))
            n = 0
            for c in range(2):
                for t in range(tiles):
                    s = slice(c * 512, (c + 1) * 512)
                    dve.wait_ge(mm["sem"], at(mm, n + 1))
                    if n >= 2:
                        dve.wait_ge(ad["sem"], at(ad, n - 1))
                    dve.tensor_tensor(prod[:, n % 2, :], core["ps"][:, n % 4, :],
                                      gr[:, 0 if t < TL else 1, s], ALU.mult).then_inc(gd["sem"], up(gd))
                    dve.wait_ge(gd["sem"], gd["total"])
                    dve.tensor_tensor(x[:, t, s], x[:, t, s], prod[:, n % 2, :],
                                      ALU.add).then_inc(ad["sem"], up(ad))
                    n += 1
    close(core)


KT_O = HO
V_O = KT_O + MH * TOK
QT_O = V_O + TT * D
T_O = QT_O + MH * LAT
OT_O = QT_O
DN_O = HO + KD * TOK
S_KPE = S_BASE
S_AN = S_BASE + 192
S_SS = S_BASE + 200
S_UP = C_TRI
S_RS = S_BASE + 216


def mla_down_stage(core, d):
    nc = core["nc"]
    ht = view(core, HO, KD, TOK)
    dn = view(core, DN_O, TT, ODD_IN)
    w = view(core, RO, KD, ODD_IN)
    sq = view(core, RO + KD * ODD_IN, QL)
    kpe = view(core, S_KPE, TT, ROPE)
    an = view(core, S_AN, 5)
    ss = view(core, S_SS, TT, 2)
    rs = view(core, S_RS, TT, 2)
    qat = view(core, T_O, 3, LAT)
    kvt = view(core, T_O + 3 * LAT, 2, TOK)
    ld = signal(core, "down_weights_loaded")
    mm = signal(core, "down_product_done")
    ev = signal(core, "down_rows_out")
    qs = signal(core, "down_squares_summed")
    st = signal(core, "down_rows_step")
    tr = signal(core, "down_rows_turned")
    co = signal(core, "down_columns_out")
    with nc.Block() as block:
        @block.sync
        def _(sp):
            sp.dma_start(w, d["l1_w_dqkv"].rearrange("(k p) n -> p k n", p=P)).then_inc(ld["sem"], up(ld, 16))
            sp.dma_start(an, d["a_norms"]).then_inc(ld["sem"], up(ld, 16))

        @block.tensor
        def _(pe):
            pe.wait_ge(ld["sem"], at(ld, 32))
            for t in range(TT):
                if t >= 2:
                    pe.wait_ge(ev["sem"], at(ev, t - 1))
                o = pair(core, 2 * (t % 2))
                for a, b in ((0, 512), (512, ODD_IN)):
                    for k in range(KD):
                        i = pe.matmul(o[:, a:b], ht[:, k, t * P:(t + 1) * P], w[:, k, a:b],
                                      start=(k == 0), stop=(k == KD - 1))
                i.then_inc(mm["sem"], up(mm))
            for t in range(TT):
                pe.wait_ge(st["sem"], at(st, 3 + 2 * t + 2))
                if t >= 2:
                    pe.wait_ge(co["sem"], at(co, t - 1))
                for k in range(5):
                    if k < 3 and t >= TL:
                        continue
                    i = pe.transpose(pair(core, 4 + 2 * (t % 2))[:, k * P:(k + 1) * P],
                                     dn[:, t, k * P:(k + 1) * P], ident(core))
                i.then_inc(tr["sem"], up(tr))

        @block.scalar
        def _(act):
            for t in range(TT):
                act.wait_ge(ev["sem"], at(ev, t + 1))
                for j, (a, b) in enumerate(((0, QL), (QL, QL + KVL))):
                    if t or j:
                        act.wait_ge(qs["sem"], qs["total"])
                    act.activation(sq[:, 0:b - a], dn[:, t, a:b], ACT.Square,
                                   accum_out=ss[:, t, j:j + 1]).then_inc(qs["sem"], up(qs))
            act.wait_ge(st["sem"], at(st, 2))
            act.activation(rs.rearrange("p a b -> p (a b)"), ss.rearrange("p a b -> p (a b)"),
                           ACT.Sqrt).then_inc(qs["sem"], up(qs))
            for t in range(TT):
                act.wait_ge(tr["sem"], at(tr, t + 1))
                for k in range(5):
                    if k < 3 and t >= TL:
                        continue
                    o = qat[:, k, t * P:(t + 1) * P] if k < 3 else kvt[:, k - 3, t * P:(t + 1) * P]
                    i = act.activation(o, pair(core, 4 + 2 * (t % 2))[:, k * P:(k + 1) * P], ACT.Copy,
                                       scale=an[:, k:k + 1])
                i.then_inc(co["sem"], up(co))

        @block.vector
        def _(dve):
            for t in range(TT):
                dve.wait_ge(mm["sem"], at(mm, t + 1))
                dve.tensor_copy(dn[:, t, :], pair(core, 2 * (t % 2))[:, 0:ODD_IN]).then_inc(ev["sem"], up(ev))
            dve.wait_ge(qs["sem"], at(qs, 2 * TT))
            dve.tensor_scalar(ss[:, :, 0:1], ss[:, :, 0:1], 1.0 / QL, EPS, ALU.mult,
                              ALU.add).then_inc(st["sem"], up(st))
            dve.tensor_scalar(ss[:, :, 1:2], ss[:, :, 1:2], 1.0 / KVL, EPS, ALU.mult,
                              ALU.add).then_inc(st["sem"], up(st))
            dve.wait_ge(qs["sem"], at(qs, 2 * TT + 1))
            dve.reciprocal(rs.rearrange("p a b -> p (a b)"),
                           rs.rearrange("p a b -> p (a b)")).then_inc(st["sem"], up(st))
            dve.wait_ge(st["sem"], st["total"])
            for t in range(TT):
                for j, (a, b) in enumerate(((0, QL), (QL, QL + KVL))):
                    dve.tensor_scalar(dn[:, t, a:b], dn[:, t, a:b], rs[:, t, j:j + 1], None,
                                      ALU.mult).then_inc(st["sem"], up(st))
            dve.wait_ge(ev["sem"], ev["total"])
            dve.tensor_copy(kpe, dn[:, :, QL + KVL:ODD_IN]).then_inc(st["sem"], up(st))
    close(core)


def mla_up_stage(core, d):
    nc = core["nc"]
    wq = view(core, RO, 3, MH * QK)
    wkv = view(core, RO + 3 * MH * QK, 2, MH * (NOPE + MV))
    rowb = view(core, RO + 8704, 2, MH * QK)
    kpe = view(core, S_KPE, TT, ROPE)
    qat = view(core, T_O, 3, LAT)
    kvt = view(core, T_O + 3 * LAT, 2, TOK)
    kt = view(core, KT_O, MH, TOK)
    qt = view(core, QT_O, MH, LAT)
    val = view(core, V_O, TT, D)
    sq = view(core, MISC, MH, QK)
    rot = view(core, MISC + MH * QK, MH, 16)
    ss = view(core, S_SS, MH)
    rs = view(core, S_RS, MH)
    gain = view(core, S_UP, 2, QK)
    cs = view(core, S_UP + 2 * QK, 2, TL * 16)
    ld = signal(core, "up_weights_loaded")
    mm = signal(core, "up_product_done")
    ev = signal(core, "up_rows_out")
    st = signal(core, "up_rows_step")
    ro = signal(core, "up_root_done")
    rd = signal(core, "up_rows_ready")
    tr = signal(core, "up_rows_turned")
    co = signal(core, "up_columns_out")
    items = []
    for t in range(TT):
        items.append((0, t))
        if t < TL:
            items.append((1, t))
    per_item = []

    count = 0
    for q, t in items:
        a = count + (3 if q else 4)
        b = a + 3 + (6 if t < TL else 0)
        per_item.append((a, b))
        count = b

    with nc.Block() as block:
        @block.sync
        def _(sp):
            sp.dma_start(wkv, d["l1_w_ukv"].rearrange("(k p) n -> p k n", p=P)).then_inc(ld["sem"], up(ld, 16))
            sp.dma_start(wq, d["l1_w_uq"].rearrange("(k p) n -> p k n", p=P)).then_inc(ld["sem"], up(ld, 16))
            sp.dma_start(view(core, S_UP, 2 * QK),
                         d["qk_norms"].to_broadcast([P, 2 * QK])).then_inc(ld["sem"], up(ld, 16))
            sp.dma_start(view(core, S_UP + 2 * QK, 2 * TL * 16), d["rope"]).then_inc(ld["sem"], up(ld, 16))

        @block.tensor
        def _(pe):
            def turn(n):
                q, t = items[n]
                pe.wait_ge(rd["sem"], at(rd, n + 1))
                if n >= 1:
                    pe.wait_ge(co["sem"], at(co, 4 * n))
                for h in range(MH):
                    i = pe.transpose(core["ps"][0:QK, 4 + h // 4, (h % 4) * P:(h % 4 + 1) * P],
                                     rowb[:, n % 2, h * QK:(h + 1) * QK], ident(core))
                    if h % 4 == 3:
                        i.then_inc(tr["sem"], up(tr))

            pe.wait_ge(ld["sem"], at(ld, 64))
            for n, (q, t) in enumerate(items):
                if n >= 1:
                    pe.wait_ge(ev["sem"], at(ev, 2 * n))
                K, a, w, C = (3, qat, wq, 3) if q else (2, kvt, wkv, 4)
                for c in range(C):
                    for k in range(K):
                        i = pe.matmul(core["ps"][:, c, :], a[:, k, t * P:(t + 1) * P],
                                      w[:, k, c * 512:(c + 1) * 512], start=(k == 0), stop=(k == K - 1))
                i.then_inc(mm["sem"], up(mm))
                if n >= 1:
                    turn(n - 1)
            turn(len(items) - 1)

        @block.scalar
        def _(act):
            def columns(n):
                q, t = items[n]
                o = qt if q else kt
                for b in range(4):
                    act.wait_ge(tr["sem"], at(tr, 4 * n + b + 1))
                    act.activation(o[0:QK, 4 * b:4 * b + 4, t * P:(t + 1) * P],
                                   core["ps"][0:QK, 4 + b, :].rearrange("p (h l) -> p h l", l=P),
                                   ACT.Copy).then_inc(co["sem"], up(co))

            for n, (q, t) in enumerate(items):
                act.wait_ge(mm["sem"], at(mm, n + 1))
                kv = core["ps"][:, 0:4, :].rearrange("p a b -> p (a b)").rearrange("p (h c) -> p h c", c=P)
                if n >= 2:
                    act.wait_ge(tr["sem"], at(tr, 4 * (n - 1)))
                row = rowb[:, n % 2, :]
                if q:
                    act.activation(row, core["ps"][:, 0:3, :].rearrange("p a b -> p (a b)"),
                                   ACT.Copy).then_inc(ev["sem"], up(ev, 2))
                else:
                    act.activation(row.rearrange("p (h c) -> p h c", c=QK)[:, :, 0:NOPE],
                                   kv[:, :, 0:NOPE], ACT.Copy).then_inc(ev["sem"], up(ev))
                    act.activation(val[:, t, :].rearrange("p (h c) -> p h c", c=MV),
                                   kv[:, :, NOPE:], ACT.Copy).then_inc(ev["sem"], up(ev))
                if n >= 1:
                    columns(n - 1)
                act.wait_ge(st["sem"], at(st, per_item[n][0]))
                act.activation(rs, ss, ACT.Sqrt).then_inc(ro["sem"], up(ro))
            columns(len(items) - 1)

        @block.vector
        def _(dve):
            dve.wait_ge(ld["sem"], at(ld, 64))
            for n, (q, t) in enumerate(items):
                row = rowb[:, n % 2, :].rearrange("p (h c) -> p h c", c=QK)
                if n >= 2:
                    dve.wait_ge(tr["sem"], at(tr, 4 * (n - 1)))
                if not q:
                    dve.tensor_copy(row[:, :, NOPE:], kpe[:, t:t + 1, :].to_broadcast([P, MH, ROPE])
                                    ).then_inc(st["sem"], up(st))
                    dve.wait_ge(st["sem"], st["total"])
                dve.wait_ge(ev["sem"], at(ev, 2 * n + 2))
                dve.tensor_tensor(sq, row, row, ALU.mult).then_inc(st["sem"], up(st))
                dve.wait_ge(st["sem"], st["total"])
                dve.tensor_reduce(ss, sq, AX_X, ALU.add).then_inc(st["sem"], up(st))
                dve.wait_ge(st["sem"], st["total"])
                dve.tensor_scalar(ss, ss, 1.0 / QK, EPS, ALU.mult, ALU.add).then_inc(st["sem"], up(st))
                dve.wait_ge(ro["sem"], at(ro, n + 1))
                dve.reciprocal(rs, rs).then_inc(st["sem"], up(st))
                dve.wait_ge(st["sem"], st["total"])
                dve.tensor_tensor(row, row, bcast(rs, QK), ALU.mult).then_inc(st["sem"], up(st))
                dve.wait_ge(st["sem"], st["total"])
                g = gain[:, 0 if q else 1:(0 if q else 1) + 1, :].to_broadcast([P, MH, QK])
                i = dve.tensor_tensor(row, row, g, ALU.mult).then_inc(st["sem"], up(st))
                if t < TL:
                    dve.wait_ge(st["sem"], st["total"])
                    x1, x2 = row[:, :, NOPE:NOPE + 16], row[:, :, NOPE + 16:]
                    c = cs[:, 0:1, t * 16:(t + 1) * 16].to_broadcast([P, MH, 16])
                    s = cs[:, 1:2, t * 16:(t + 1) * 16].to_broadcast([P, MH, 16])
                    sc = sq.rearrange("p a b -> p (a b)")
                    x1s = sc[:, 0:256].rearrange("p (h c) -> p h c", c=16)
                    x2c = sc[:, 256:512].rearrange("p (h c) -> p h c", c=16)
                    dve.tensor_tensor(rot, x2, s, ALU.mult).then_inc(st["sem"], up(st))
                    dve.tensor_tensor(x1s, x1, s, ALU.mult).then_inc(st["sem"], up(st))
                    dve.tensor_tensor(x2c, x2, c, ALU.mult).then_inc(st["sem"], up(st))
                    dve.wait_ge(st["sem"], st["total"])
                    dve.tensor_tensor(x1, x1, c, ALU.mult).then_inc(st["sem"], up(st))
                    dve.tensor_tensor(x2, x1s, x2c, ALU.add).then_inc(st["sem"], up(st))
                    dve.wait_ge(st["sem"], st["total"])
                    dve.tensor_tensor(x1, x1, rot, ALU.subtract).then_inc(st["sem"], up(st))
                assert st["total"] - st["base"] == per_item[n][1]
                dve.wait_ge(st["sem"], st["total"])
                dve.tensor_copy(rot[:, 0, 0:1], row[:, 0, 0:1]).then_inc(rd["sem"], up(rd))
    close(core)


def attention_stage(core, d):
    nc = core["nc"]
    kt = view(core, KT_O, MH, TOK)
    qt = view(core, QT_O, MH, LAT)
    val = view(core, V_O, TT, D)
    rows = view(core, RO, TL, D)
    ot = view(core, OT_O, KD, LAT)
    pr = view(core, T_O, 3, TOK)
    pt = view(core, MISC, 2, TOK)
    N = MH * TL
    top, nm, sm, rc = (view(core, S_SS + i * N, N) for i in range(4))
    sc = signal(core, "scores_ready")
    mx = signal(core, "score_peak_ready")
    ex = signal(core, "exponentials_ready")
    iv = signal(core, "softmax_sum_inverted")
    tr = signal(core, "exponentials_turned")
    pc = signal(core, "turned_exponentials_out")
    pv = signal(core, "head_output_ready")
    oo = signal(core, "head_output_out")
    tt = signal(core, "output_rows_turned")
    to = signal(core, "output_columns_out")
    scale = QK ** -0.5
    with nc.Block() as block:
        @block.tensor
        def _(pe):
            def score(n):
                h, q = divmod(n, TL)
                if n >= 2:
                    pe.wait_ge(ex["sem"], at(ex, n - 1))
                o = pair(core, 2 * (n % 2))
                for a, b in ((0, 512), (512, TOK)):
                    i = pe.matmul(o[:, a:b], qt[0:QK, h, q * P:(q + 1) * P], kt[0:QK, h, a:b],
                                  start=True, stop=True)
                i.then_inc(sc["sem"], up(sc))

            def turn(n):
                pe.wait_ge(ex["sem"], at(ex, n + 1))
                if n >= 1:
                    pe.wait_ge(pc["sem"], at(pc, n))
                for t in range(TT):
                    i = pe.transpose(pair(core, 4)[:, t * P:(t + 1) * P], pr[:, n % 3, t * P:(t + 1) * P],
                                     ident(core))
                i.then_inc(tr["sem"], up(tr))

            def weigh(n):
                h, q = divmod(n, TL)
                pe.wait_ge(pc["sem"], at(pc, n + 1))
                if n >= 2:
                    pe.wait_ge(oo["sem"], at(oo, n - 1))
                for t in range(TT):
                    i = pe.matmul(core["ps"][:, 6 + n % 2, 0:MV], pt[:, n % 2, t * P:(t + 1) * P],
                                  val[:, t, h * MV:(h + 1) * MV], start=(t == 0), stop=(t == TT - 1))
                i.then_inc(pv["sem"], up(pv))

            for n in range(N + 3):
                if n < N:
                    score(n)
                if 2 <= n < N + 2:
                    turn(n - 2)
                if n >= 3:
                    weigh(n - 3)
            pe.wait_ge(oo["sem"], at(oo, N))
            for t in range(TL):
                if t >= 2:
                    pe.wait_ge(to["sem"], at(to, t - 1))
                for k in range(KD):
                    i = pe.transpose(pair(core, 2 * (t % 2))[:, k * P:(k + 1) * P],
                                     rows[:, t, k * P:(k + 1) * P], ident(core))
                i.then_inc(tt["sem"], up(tt))

        @block.vector
        def _(dve):
            def peak(n):
                dve.wait_ge(sc["sem"], at(sc, n + 1))
                dve.tensor_reduce(top[:, n:n + 1], pair(core, 2 * (n % 2))[:, 0:TOK], AX_X,
                                  ALU.max).then_inc(mx["sem"], up(mx))
                dve.wait_ge(mx["sem"], mx["total"])
                dve.tensor_scalar(nm[:, n:n + 1], top[:, n:n + 1], -scale, None,
                                  ALU.mult).then_inc(mx["sem"], up(mx))

            def out(n):
                h, q = divmod(n, TL)
                dve.reciprocal(rc[:, n:n + 1], sm[:, n:n + 1]).then_inc(iv["sem"], up(iv))
                dve.wait_ge(iv["sem"], iv["total"])
                dve.wait_ge(pv["sem"], at(pv, n + 1))
                dve.tensor_scalar(rows[:, q, h * MV:(h + 1) * MV], core["ps"][:, 6 + n % 2, 0:MV],
                                  rc[:, n:n + 1], None, ALU.mult).then_inc(oo["sem"], up(oo))

            for n in range(N + 4):
                if n < N:
                    peak(n)
                if n >= 4:
                    dve.wait_ge(ex["sem"], at(ex, n - 3))
                    out(n - 4)

        @block.scalar
        def _(act):
            for n in range(N + 2):
                if n < N:
                    act.wait_ge(mx["sem"], at(mx, 2 * (n + 1)))
                    if n >= 3:
                        act.wait_ge(tr["sem"], at(tr, n - 2))
                    act.activation(pr[:, n % 3, :], pair(core, 2 * (n % 2))[:, 0:TOK], ACT.Exp,
                                   bias=nm[:, n:n + 1], scale=scale,
                                   accum_out=sm[:, n:n + 1]).then_inc(ex["sem"], up(ex))
                if n >= 2:
                    u = n - 2
                    act.wait_ge(tr["sem"], at(tr, u + 1))
                    if u >= 2:
                        act.wait_ge(pv["sem"], at(pv, u - 1))
                    act.activation(pt[:, u % 2, :], pair(core, 4)[:, 0:TOK],
                                   ACT.Copy).then_inc(pc["sem"], up(pc))
            for t in range(TL):
                act.wait_ge(tt["sem"], at(tt, t + 1))
                act.activation(ot[:, :, t * P:(t + 1) * P],
                               pair(core, 2 * (t % 2)).rearrange("p (k l) -> p k l", l=P),
                               ACT.Copy).then_inc(to["sem"], up(to))
    close(core)


H2_O = L0
ROWS = 2 * D
LATE_O = H2_O + TT * D
W_O = LATE_O + 6 * ROWS
BATCH = 4
NB = TOPK // BATCH
HW = PQ
SIDE = PQ // 2


def peer_slots(tiles):
    early = [RO + n * ROWS for n in range(6)] + [LATE_O + n * ROWS for n in range(6)]
    if tiles == TT:
        return early
    return early + [H2_O + TL * D, XO + TL * D, HO + KD * LAT, WORDS - ROWS]


def peer_stage(core, d, layer, tiles):
    nc = core["nc"]
    steps = tiles * PH
    n_tok = tiles * P
    starts = peer_slots(tiles)
    NS = len(starts)
    USES = tiles * TOPK // NS
    assert tiles % 2 == 0 and USES * NS == tiles * TOPK
    slots = [view(core, o, ROWS) for o in starts]
    x = view(core, XO, TT, D)
    h2 = view(core, H2_O, TT, D)
    ht = view(core, HO, KD, n_tok)
    top = [W_O]

    def take(*shape):
        n = 1
        for s in shape:
            n *= s
        v = view(core, top[0], *shape)
        top[0] += n
        return v

    g2 = take(2 if tiles > TL else 1, D)
    diag = take(BATCH * 2, P)
    wq = take(KD, SIDE)
    keys = take(2, PK)
    sc = take(tiles, 2, PK)
    qb = take(n_tok)
    hot = take(2 * TOPK, TOPK)
    best = take(2, TOPK)
    where = take(2, TOPK).bitcast(U32)
    wheref = take(2, TOPK)
    score = take(TOPK)
    pick = take(TOPK).bitcast(U32)
    halves = take(2, TOPK).bitcast(U32)
    halvesf = take(2, TOPK)
    ef = take(2 * TOPK)
    shifted = take(TOPK)
    raised = take(TOPK)
    total = take(2)
    dots = take(TOPK)
    gel = take(TOPK)
    wts = take(TOPK)
    expert = take(2, TOPK).bitcast(U32)
    gate = take(2, TOPK)
    assert top[0] <= (WORDS if tiles > TL else WORDS - ROWS)
    rest = view(core, C_TRI, 2, PK)
    cand = view(core, C_TRI + 2 * PK, TOPK, TOPK)
    cand2 = view(core, C_TRI + 4 * PK, TOPK, TOPK)
    assert C_TRI + 6 * PK <= C_IOTA
    iota = view(core, C_IOTA, TOPK)
    flat = lambda v: v.rearrange("p a b -> p (a b)")
    sig = lambda name: signal(core, name)
    g2l = sig("peer_gates_loaded")
    wql = sig("peer_wq_loaded")
    kyl = sig("peer_keys_loaded")
    qmm = sig("peer_query_done")
    qev = sig("peer_query_out")
    smm = sig("peer_scores_done")
    sev = sig("peer_scores_out")
    rdy = sig("peer_experts_chosen")
    cho = sig("peer_choice_step")
    ctn = sig("peer_choice_turn")
    gtd = sig("peer_step_gates_ready")
    scd = sig("peer_scores_copied")
    exd = sig("peer_softmax_raised")
    turn = sig("peer_gather_turn")
    zero = sig("peer_diagonals_zeroed")
    free = sig("peer_slot_used")
    land = [sig(f"peer_slot{s}_landed") for s in range(NS)]
    dot = sig("peer_dots_ready")
    gl = sig("peer_gelu_ready")
    wt = sig("peer_weights_ready")
    dg = sig("peer_diagonals_ready")
    rd = sig("peer_step_read")
    xup = sig("peer_step_added")
    CHA, CH = 17, 25
    tbl = d[f"experts{layer}"]
    wq_d = d[f"wq{layer}"].rearrange("(k p) n -> p k n", p=P)
    keys_d = d[f"keys{layer}"]

    with nc.Block() as block:
        @block.sync
        def _(sp):
            def load_side(col):
                sp.dma_start(wq, wq_d[:, :, bass.ds(col, SIDE)]).then_inc(wql["sem"], 16)

            def load_keys(h):
                sp.dma_start(flat(keys), keys_d[:, bass.ds(h * 2 * PK, 2 * PK)]).then_inc(kyl["sem"], 16)

            load_side(0)
            load_keys(0)
            for n in range(g2.shape[1]):
                sp.dma_start(g2[:, n, :].rearrange("p (k l) -> p k l", l=P),
                             gate_rows(core, layer, 1, n)).then_inc(g2l["sem"], up(g2l, 16))
            sp.wait_ge(qmm["sem"], at(qmm, 1))
            load_side(SIDE)
            with sp.Fori(0, PH) as h:
                sp.wait_ge(qmm["sem"], h * 2 + at(qmm, 2))
                load_side(h * HW + HW)
                sp.wait_ge(smm["sem"], h * 2 + at(smm, 2))
                load_keys(h + 1)
                sp.wait_ge(qmm["sem"], h * 2 + at(qmm, 3))
                load_side(h * HW + HW + SIDE)
            sp.wait_ge(wql["sem"], at(wql, 32 * (PH + 1)))
            sp.wait_ge(kyl["sem"], at(kyl, 16 * (PH + 1)))

        @block.gpsimd
        def _(pool):
            with pool.Fori(0, PH) as h:
                for t in range(tiles):
                    i = h * tiles + t
                    pool.wait_ge(rdy["sem"], i + at(rdy, 1))
                    for k in range(TOPK):
                        s = (t * TOPK + k) % NS
                        pool.wait_ge(free["sem"], i * TOPK + at(free, k + 1))
                        pool.sem_inc(turn["sem"], 1)
                        pool.indirect_dma_start(slots[s], None, tbl,
                                                bass.IndirectOffsetOnAxis(ap=expert[:, t % 2, k:k + 1], axis=0)
                                                ).then_inc(land[s]["sem"], 16)

        @block.tensor
        def _(pe):
            def query(side, part, k0, k1, n2):
                a, b = ((0, 512), (512, n_tok))[part]
                if k0 == 0 and part == 0:
                    pe.wait_ge(wql["sem"], n2 * 16 + at(wql, 16 * (side + 1)))
                    if side == 1:
                        pe.wait_ge(qev["sem"], n2 + at(qev, 1))
                for k in range(k0, k1):
                    mm = pe.matmul(pair(core, 4)[:, a:b], wq[:, k, :], ht[:, k, a:b],
                                   start=(k == 0), stop=(k == KD - 1))
                if k1 == KD and b == n_tok:
                    mm.then_inc(qmm["sem"], 1)

            def scores(side, n2):
                if side == 0:
                    pe.wait_ge(kyl["sem"], n2 * 8 + at(kyl, 16))
                pe.wait_ge(qev["sem"], n2 + at(qev, side + 1))
                for t in range(tiles):
                    mm = pe.matmul(pair(core, 6 - 2 * side)[:, t * P:(t + 1) * P],
                                   qb[:, t * P:(t + 1) * P], keys[:, side, :], start=True, stop=True)
                mm.then_inc(smm["sem"], 1)

            def ahead(h, t, b):
                n2 = h * 2 + 2
                where_in = t * NB + b
                if where_in == 0:
                    pe.wait_ge(sev["sem"], h + at(sev, 1))
                    query(0, 0, 0, 4, n2)
                if where_in == 1:
                    query(0, 0, 4, 8, n2)
                if where_in == 2 and n_tok > 512:
                    query(0, 1, 0, 8, n2)
                if where_in == 4:
                    scores(0, n2)
                if where_in == 5:
                    query(1, 0, 0, 4, n2)
                if where_in == 6:
                    query(1, 0, 4, 8, n2)
                if where_in == 7 and n_tok > 512:
                    query(1, 1, 0, 8, n2)
                if where_in == 9:
                    scores(1, n2)

            pe.wait_ge(zero["sem"], at(zero, 1))
            for c in range(2):
                mm = pe.matmul(core["ps"][:, 2 + c, :], diag[:, 0, :], flat(diag[:, 0:4, :]), start=True, stop=True)
            mm.then_inc(free["sem"], NS)
            for side in range(2):
                query(side, 0, 0, 8, 0)
                if n_tok > 512:
                    query(side, 1, 0, 8, 0)
                scores(side, 0)
            with pe.Fori(0, PH) as h:
                for t in range(tiles):
                    i = h * tiles + t
                    pe.wait_ge(rd["sem"], i + at(rd, 1))
                    for b in range(NB):
                        pe.wait_ge(dg["sem"], i * NB + at(dg, NB + b + 1))
                        for k in range(b * BATCH, (b + 1) * BATCH):
                            v = slots[(t * TOPK + k) % NS]
                            for c in range(2):
                                mm = pe.matmul(core["ps"][:, 2 * (t % 2) + c, :], diag[:, k % (2 * BATCH), :],
                                               v[:, D + c * 512:D + (c + 1) * 512],
                                               start=(k == 0), stop=(k == TOPK - 1))
                            mm.then_inc(free["sem"], 1)
                        ahead(h, t, b)

        @block.scalar
        def _(act):
            def softmax(n):
                act.wait_ge(cho["sem"], n)
                act.activation(raised, shifted, ACT.Exp, accum_out=total[:, 0:1]).then_inc(exd["sem"], 1)

            def query_out(side, n2, first=False):
                if not (first and side == 0):
                    act.wait_ge(smm["sem"], n2 + at(smm, side))
                act.wait_ge(qmm["sem"], n2 + at(qmm, side + 1))
                act.activation(qb, pair(core, 4)[:, 0:n_tok], ACT.Copy).then_inc(qev["sem"], 1)

            act.sem_inc(dg["sem"], NB)
            query_out(0, 0, True)
            query_out(1, 0)
            softmax(at(cho, CHA))
            with act.Fori(0, PH) as h:
                for t in range(tiles):
                    i = h * tiles + t
                    for b in range(NB):
                        s = slice(b * BATCH, (b + 1) * BATCH)
                        act.wait_ge(dot["sem"], i * TOPK + at(dot, (b + 1) * BATCH))
                        act.activation(gel[:, s], dots[:, s], ACT.Gelu).then_inc(gl["sem"], 1)
                        if b == 0:
                            softmax(i * CH + at(cho, CH + CHA))
                        act.wait_ge(free["sem"], i * TOPK + at(free, NS - BATCH + b * BATCH))
                        act.wait_ge(wt["sem"], i * NB + at(wt, b + 1))
                        for k in range(b * BATCH, (b + 1) * BATCH):
                            ins = act.activation(diag[:, k % (2 * BATCH), :], ident(core), ACT.Copy,
                                                 scale=wts[:, k:k + 1])
                        ins.then_inc(dg["sem"], 1)
                        if t * NB + b == 3:
                            query_out(0, h * 2 + 2)
                        if t * NB + b == 8:
                            query_out(1, h * 2 + 2)

        @block.vector
        def _(dve):
            def choose_a(cur, first):
                for s in range(2):
                    dve.max(best[:, s, 0:8], cur[:, s, :]).then_inc(cho["sem"], 1)
                dve.wait_ge(cho["sem"], first + 2)
                dve.sem_inc(ctn["sem"], 1)
                for s in range(2):
                    dve.max_index(where[:, s, 0:8], best[:, s, 0:8], cur[:, s, :]).then_inc(cho["sem"], 1)
                    dve.match_replace(rest[:, s, :], best[:, s, 0:8], cur[:, s, :],
                                      LOWEST).then_inc(cho["sem"], 1)
                dve.wait_ge(cho["sem"], first + 6)
                dve.sem_inc(ctn["sem"], 1)
                for s in range(2):
                    dve.max(best[:, s, 8:16], rest[:, s, :]).then_inc(cho["sem"], 1)
                dve.wait_ge(cho["sem"], first + 8)
                dve.sem_inc(ctn["sem"], 1)
                for s in range(2):
                    dve.max_index(where[:, s, 8:16], best[:, s, 8:16], rest[:, s, :]).then_inc(cho["sem"], 1)
                dve.tensor_tensor(cand, bcast(best[:, 0, :], TOPK),
                                  best[:, 1:2, :].to_broadcast([P, TOPK, TOPK]), ALU.add).then_inc(cho["sem"], 1)
                dve.wait_ge(cho["sem"], first + 11)
                dve.sem_inc(ctn["sem"], 1)
                dve.max(score[:, 0:8], flat(cand)).then_inc(cho["sem"], 1)
                dve.wait_ge(cho["sem"], first + 12)
                dve.sem_inc(ctn["sem"], 1)
                dve.max_index(pick[:, 0:8], score[:, 0:8], flat(cand)).then_inc(cho["sem"], 1)
                dve.match_replace(flat(cand2), score[:, 0:8], flat(cand), LOWEST).then_inc(cho["sem"], 1)
                dve.wait_ge(cho["sem"], first + 14)
                dve.sem_inc(ctn["sem"], 1)
                dve.max(score[:, 8:16], flat(cand2)).then_inc(cho["sem"], 1)
                dve.wait_ge(cho["sem"], first + 15)
                dve.sem_inc(ctn["sem"], 1)
                dve.max_index(pick[:, 8:16], score[:, 8:16], flat(cand2)).then_inc(cho["sem"], 1)
                dve.tensor_scalar(shifted, score, score[:, 0:1], None, ALU.subtract).then_inc(cho["sem"], 1)

            def choose_b(i, par, first):
                dve.tensor_copy(flat(wheref), flat(where)).then_inc(cho["sem"], 1)
                dve.wait_ge(cho["sem"], first + 17)
                dve.tensor_scalar(halves[:, 0, :], pick, 4, None, ALU.logical_shift_right).then_inc(cho["sem"], 1)
                dve.tensor_scalar(halves[:, 1, :], pick, 15, None, ALU.bitwise_and).then_inc(cho["sem"], 1)
                dve.wait_ge(cho["sem"], first + 20)
                dve.tensor_copy(flat(halvesf), flat(halves)).then_inc(cho["sem"], 1)
                dve.wait_ge(cho["sem"], first + 21)
                dve.tensor_tensor(hot, bcast(flat(halvesf), TOPK),
                                  iota.unsqueeze(1).to_broadcast([P, 2 * TOPK, TOPK]),
                                  ALU.is_equal).then_inc(cho["sem"], 1)
                dve.wait_ge(cho["sem"], first + 22)
                hot4 = hot.rearrange("p (s k) j -> p s k j", s=2)
                dve.tensor_tensor(hot4, hot4, wheref.unsqueeze(2).to_broadcast([P, 2, TOPK, TOPK]),
                                  ALU.mult).then_inc(cho["sem"], 1)
                dve.wait_ge(exd["sem"], i + at(exd, 1))
                dve.reciprocal(total[:, 1:2], total[:, 0:1]).then_inc(cho["sem"], 1)
                dve.wait_ge(cho["sem"], first + 24)
                dve.tensor_scalar(gate[:, par, :], raised, total[:, 1:2], None, ALU.mult).then_inc(gtd["sem"], 1)
                dve.tensor_reduce(ef, hot, AX_X, ALU.add).then_inc(cho["sem"], 1)
                dve.wait_ge(cho["sem"], first + 25)
                dve.scalar_tensor_tensor(out=expert[:, par, :], in0=ef[:, 0:TOPK], scalar=float(PK),
                                         in1=ef[:, TOPK:2 * TOPK], op0=ALU.mult,
                                         op1=ALU.add).then_inc(rdy["sem"], 1)

            def scores_out(n2):
                for side in range(2):
                    dve.wait_ge(smm["sem"], n2 + at(smm, side + 1))
                    dve.tensor_copy(sc[:, :, side, :],
                                    pair(core, 6 - 2 * side)[:, 0:n_tok].rearrange("p (t k) -> p t k", k=PK)
                                    ).then_inc(scd["sem"], 1)

            def dot_batch(h, t, i, b):
                for k in range(b * BATCH, (b + 1) * BATCH):
                    use, s = divmod(t * TOPK + k, NS)
                    dve.wait_ge(land[s]["sem"], h * 16 * USES + at(land[s], 16 * (use + 1)))
                    u = slots[s][:, 0:D]
                    dve.tensor_tensor_reduce(u, u, h2[:, t, :], 1.0, 0.0, ALU.mult, ALU.add,
                                             dots[:, k:k + 1]).then_inc(dot["sem"], 1)

            def weigh(i, par, b):
                s = slice(b * BATCH, (b + 1) * BATCH)
                dve.wait_ge(dg["sem"], i * NB + at(dg, b + 1))
                dve.wait_ge(gl["sem"], i * NB + at(gl, b + 1))
                dve.tensor_tensor(wts[:, s], gel[:, s], gate[:, par, s], ALU.mult).then_inc(wt["sem"], 1)

            def add_step(i, t):
                dve.wait_ge(free["sem"], i * TOPK + at(free, NS))
                banks = pair(core, 2 * (t % 2))
                dve.tensor_tensor(banks, banks, g2[:, 0 if t < TL else 1, :], ALU.mult).then_inc(xup["sem"], 1)
                dve.wait_ge(xup["sem"], i + at(xup, 1))
                dve.tensor_tensor(x[:, t, :], x[:, t, :], banks, ALU.add).then_inc(rd["sem"], 1)

            dve.memset(flat(diag[:, :, :]), 0.0).then_inc(zero["sem"], up(zero))
            dve.sem_inc(rd["sem"], 1)
            dve.wait_ge(g2l["sem"], g2l["total"])
            scores_out(0)
            dve.wait_ge(scd["sem"], at(scd, 2))
            dve.sem_inc(sev["sem"], 1)
            choose_a(sc[:, 0, :, :], at(cho, 0))
            choose_b(0, 0, at(cho, 0))
            with dve.Fori(0, PH) as h:
                for t in range(tiles):
                    i = h * tiles + t
                    done = i * CH + at(cho, CH)
                    dot_batch(h, t, i, 0)
                    dve.wait_ge(gtd["sem"], i + at(gtd, 1))
                    dve.sem_inc(ctn["sem"], 1)
                    if t == tiles - 1:
                        scores_out(h * 2 + 2)
                        dve.wait_ge(scd["sem"], h * 2 + at(scd, 4))
                        dve.sem_inc(sev["sem"], 1)
                    choose_a(sc[:, (t + 1) % tiles, :, :], done)
                    weigh(i, t % 2, 0)
                    dot_batch(h, t, i, 1)
                    choose_b(i + 1, 1 - t % 2, done)
                    weigh(i, t % 2, 1)
                    dot_batch(h, t, i, 2)
                    add_step(i, (t - 1) % tiles)
                    weigh(i, t % 2, 2)
                    dot_batch(h, t, i, 3)
                    weigh(i, t % 2, 3)
            add_step(steps, tiles - 1)
    up(wql, 32 * (PH + 1))
    up(kyl, 16 * (PH + 1))
    for s in (qmm, qev, smm, scd):
        up(s, 2 * (PH + 1))
    up(sev, PH + 1)
    for s in (rdy, exd, gtd):
        up(s, steps + 1)
    up(cho, (steps + 1) * CH)
    up(ctn, 7 * (steps + 1) + steps)
    up(turn, steps * TOPK)
    up(free, NS + steps * TOPK)
    for s in land:
        up(s, 16 * USES * PH)
    up(dot, steps * TOPK)
    up(gl, steps * NB)
    up(wt, steps * NB)
    up(dg, NB + steps * NB)
    up(rd, 2 + steps)
    up(xup, 1 + steps)
    close(core)


def store_stage(core, d):
    nc = core["nc"]
    st = signal(core, "output_stored")
    with nc.Block() as block:
        @block.sync
        def _(sp):
            sp.dma_start(d["out"].rearrange("(t p) n -> p t n", p=P),
                         view(core, XO, TL, D)).then_inc(st["sem"], up(st, 16))
            sp.wait_ge(st["sem"], at(st, 16))
    close(core)


def program(nc, d, stages):
    with ExitStack() as ctx:
        core = {"nc": nc, "ctx": ctx, "signals": {}, "gates": d["gates"],
                "sb": ctx.enter_context(nc.sbuf_tensor("arena", [P, WORDS], F32)),
                "ps": ctx.enter_context(nc.psum_tensor("banks", [P, 8, 512], F32))}
        core["ring"] = [signal(core, f"ring_slot{s}_loaded") for s in range(3)]
        load_constants(core, d)
        if "ada0" in stages:
            ada_stage(core, d)
        if "mix0" in stages:
            norm_stage(core, 0, 0, TT)
            project_stage(core, d)
            fourier_stage(core, d)
            ssd_stage(core, d)
            gate_stage(core, d)
            ft = view(core, FT_O, GROUPS, TOK)
            ms = view(core, BC_O, KD, TOK)
            col = lambda k, t: (ft[:, k, t * P:(t + 1) * P] if k < GROUPS
                                else ms[:, k - GROUPS, t * P:(t + 1) * P])
            out_stage(core, d["l0_w_out"], col, lambda c: view(core, RO + c * 6144, EVEN_OUT // P, 512),
                      XS_O, 0, TT)
        if "peer0" in stages:
            norm_stage(core, 0, 1, TT, view(core, H2_O, TT, D))
            peer_stage(core, d, 0, TT)
        if "mix1" in stages:
            norm_stage(core, 1, 0, TT)
            mla_down_stage(core, d)
            mla_up_stage(core, d)
            attention_stage(core, d)
            ot = view(core, OT_O, KD, LAT)
            out_stage(core, d["l1_w_o"], lambda k, t: ot[:, k, t * P:(t + 1) * P],
                      lambda c: view(core, RO + (c + 1) * SLOT, KD, 512), KT_O, 1, TL)
        if "peer1" in stages:
            norm_stage(core, 1, 1, TL, view(core, H2_O, TT, D))
            peer_stage(core, d, 1, TL)
        store_stage(core, d)


ALL = ("ada0", "mix0", "peer0", "mix1", "peer1")


def shape_constants():
    import numpy as np

    const = np.zeros((P, C_WORDS), np.float32)
    const[:, C_ID:C_ID + P] = np.eye(P)
    k, l = np.meshgrid(np.arange(P), np.arange(P), indexing="ij")
    const[:, C_TRI:C_TRI + P] = k <= l
    const[:, C_TRI + P:C_TRI + 2 * P] = k >= l
    const_bf = np.concatenate([np.eye(P), np.where(k > l, -1e30, 0), np.where(k < l, -1e30, 0)], 1)
    const_bf = (const_bf.astype(np.float32).view(np.uint32) >> 16).astype(np.uint16).view(np.float32)
    const[:, C_ONE:C_ONE + P] = 1

    def dft(n, sign):
        a = 2 * np.pi * ((np.arange(n)[:, None] * np.arange(n)[None, :]) % n) / n
        return np.concatenate([np.cos(a), sign * np.sin(a)], 1) / np.sqrt(n)

    const[:, C_DFT:C_DFT + 2 * P] = dft(GDIM, 1.0)
    const[:, C_IOTA:C_IOTA + TOPK] = np.arange(TOPK)
    rows, cols = np.repeat(np.arange(LAT // 64), 64), np.arange(LAT) % 64
    inv = (np.float32(10000.0) ** (-np.arange(0, 16, 2, dtype=np.float32) / np.float32(16))).astype(np.float32)
    ang = np.concatenate([rows[:, None].astype(np.float32) * inv, cols[:, None].astype(np.float32) * inv], 1)
    rope = np.stack([np.cos(ang), np.sin(ang)], 0).astype(np.float32)
    rope = rope.reshape(2, TL, P, 16).transpose(2, 0, 1, 3).reshape(P, 2 * TL * 16)
    return {"const": const, "const_bf": const_bf, "dft_lat": dft(LAT, -1.0).astype(np.float32),
            "dft_ctx": dft(CTX, -1.0).astype(np.float32), "rope": np.ascontiguousarray(rope)}


def kernel(**inputs):
    import numpy as np
    import concourse.bacc as bacc
    from concourse.bass_utils import run_bass_kernel_spmd

    a = {k: np.asarray(v) for k, v in inputs.items()}
    col = lambda v: v.reshape(-1, P).T
    arrays = dict(shape_constants())
    arrays["x"] = a["x"].reshape(LAT, D)
    arrays["ctx"] = a["ctx"].reshape(CTX, D)
    arrays["cond"] = np.stack([col(a["c"][0]), col(a["c_ctx"])], 2).reshape(P, 2 * KD)
    arrays["norms"] = np.concatenate([col(a[f"l{i}_norm{j}"]) for i in range(2) for j in (1, 2)], 1)
    for i in range(2):
        arrays[f"l{i}_w_ada"] = a[f"l{i}_w_ada"]
        w = a[f"l{i}_peer_wq"]
        arrays[f"wq{i}"] = np.concatenate([w, w[:, 0:HW]], 1)
        keys = a[f"l{i}_peer_keys"].transpose(3, 0, 1, 2).reshape(P, 2 * PH * PK)
        arrays[f"keys{i}"] = np.concatenate([keys, keys[:, 0:2 * PK]], 1)
        arrays[f"experts{i}"] = np.concatenate([a[f"l{i}_peer_u"], a[f"l{i}_peer_v"]], 1)
    arrays["ada_bias"] = np.concatenate([col(a[f"l{i}_b_ada"]) for i in range(2)], 1)
    arrays["l0_w_in"] = a["l0_w_in"]
    arrays["conv"] = np.concatenate([a["l0_conv_w"].reshape(TAPS, 16, P).transpose(2, 1, 0).reshape(P, 80),
                                     col(a["l0_conv_b"])], 1)
    arrays["ssd_rows"] = np.concatenate([a["l0_dt_bias"].reshape(1, 32), a["l0_a_log"].reshape(1, 32),
                                         a["l0_d_skip"].reshape(1, 32)], 1)
    arrays["ssd_norm"] = col(a["l0_ssd_norm"])
    arrays["l0_w_out"] = a["l0_w_out"]
    arrays["a_norms"] = np.concatenate([col(a["l1_q_a_norm"]), col(a["l1_kv_a_norm"])], 1)
    arrays["qk_norms"] = np.concatenate([a["l1_q_norm"], a["l1_k_norm"]]).reshape(1, 2 * QK)
    for n in ("l1_w_dqkv", "l1_w_uq", "l1_w_ukv", "l1_w_o"):
        arrays[n] = a[n]
    arrays = {k: np.ascontiguousarray(v) for k, v in arrays.items()}
    nc = bacc.Bacc("TRN2", target_bir_lowering=False, num_devices=1)
    d = {k: nc.dram_tensor(k, v.shape, F32, kind="ExternalInput").ap() for k, v in arrays.items()}
    d["gates"] = nc.dram_tensor("gates", (2, 2, 2 * KD, P), F32, kind="Internal").ap()
    d["out"] = nc.dram_tensor("out", (LAT, D), F32, kind="ExternalOutput").ap()
    program(nc, d, ALL)
    r = run_bass_kernel_spmd(nc, [arrays], core_ids=[0])
    return r.results[0]["out"].reshape(1, LAT, D)
```
